# Optimizing a Trainium2 kernel written in Bass

```python
import math
import jax, jax.numpy as jnp
from jax import lax
import numpy as np

D_MODEL = 1024
BATCH = 1
SEQ = 256
DEPTH = 4

N_MIXERS = 3
N_META = 16
BLOCK_Q = 128
RMS_EPS = 1e-6
SB_HEADS = 8
SB_HEAD_DIM = D_MODEL // SB_HEADS
SB_SCALE = 1.0 / math.sqrt(SB_HEAD_DIM)
MLA_HEADS = 8
MLA_NOPE_DIM = 128
MLA_ROPE_DIM = 64
MLA_V_DIM = 128
MLA_Q_RANK = 3 * D_MODEL // 8
MLA_KV_RANK = D_MODEL // 4
MLA_SCALE = 1.0 / math.sqrt(MLA_NOPE_DIM + MLA_ROPE_DIM)
ROPE_THETA = 10000.0
RW_HEAD_DIM = 64
RW_HEADS = D_MODEL // RW_HEAD_DIM
RW_DECAY_LORA = 64
RW_A_LORA = 64
RW_GATE_LORA = 160
RW_LN_EPS = 64e-5
D_FF = ((8 * D_MODEL // 3 + 127) // 128) * 128
N_SB = (DEPTH + 2) // 3
N_MLA = (DEPTH + 1) // 3
N_RWKV = DEPTH // 3

kernel_name = 'hybrid_sb_mla_rwkv7_macaron'

def _rmsnorm(x, g):
    xf = x.astype(jnp.float32)
    y = xf * lax.rsqrt(jnp.mean(xf * xf, axis=-1, keepdims=True) + RMS_EPS)
    return (y * g.astype(jnp.float32)).astype(x.dtype)

def _swiglu(h, w_in, w_out):
    gate, up = jnp.split(h @ w_in, 2, axis=-1)
    return (jax.nn.silu(gate) * up) @ w_out

def _query_blocks(length):
    blocks = [(0, N_META)]
    for q0 in range(N_META, length, BLOCK_Q):
        blocks.append((q0, min(BLOCK_Q, length - q0)))
    return blocks

def _block_sweep(q, k, v, block_fn):
    outs = []
    for q0, tq in _query_blocks(q.shape[2]):
        tk = q0 + tq
        outs.append(block_fn(q[:, :, q0:q0 + tq], k[:, :, :tk], v[:, :, :tk], q0))
    return jnp.concatenate(outs, axis=2)

def _stick_breaking_block(qb, kp, vp, q0):
    tq, tk = qb.shape[2], kp.shape[2]
    nkb = -(-tk // BLOCK_Q)
    pad = nkb * BLOCK_Q - tk
    kp = jnp.pad(kp, ((0, 0), (0, 0), (0, pad), (0, 0)))
    vp = jnp.pad(vp, ((0, 0), (0, 0), (0, pad), (0, 0)))
    z = jnp.einsum('bhqd,bhkd->bhqk', qb, kp).astype(jnp.float32)
    valid = jnp.arange(nkb * BLOCK_Q)[None, :] < (q0 + jnp.arange(tq))[:, None]
    log_1m = jnp.where(valid, -jax.nn.softplus(z), 0.0)
    lb = log_1m.reshape(log_1m.shape[0], log_1m.shape[1], tq, nkb, BLOCK_Q)
    idx = jnp.arange(BLOCK_Q)
    incl = (idx[:, None] >= idx[None, :]).astype(jnp.float32)
    within = jnp.einsum('bhqnk,kj->bhqnj', lb, incl)
    bidx = jnp.arange(nkb)
    later = (bidx[:, None] > bidx[None, :]).astype(jnp.float32)
    carry = jnp.einsum('bhqn,nm->bhqm', within[..., 0], later)
    r = (within + carry[..., None]).reshape(z.shape)
    a = jnp.where(valid, jnp.exp(z + r), 0.0)
    return jnp.einsum('bhqk,bhkd->bhqd', a.astype(vp.dtype), vp)

def _softmax_block(qb, kp, vp, q0):
    tq, tk = qb.shape[2], kp.shape[2]
    z = jnp.einsum('bhqd,bhkd->bhqk', qb, kp).astype(jnp.float32) * MLA_SCALE
    valid = jnp.arange(tk)[None, :] <= (q0 + jnp.arange(tq))[:, None]
    p = jax.nn.softmax(jnp.where(valid, z, -jnp.inf), axis=-1)
    return jnp.einsum('bhqk,bhkd->bhqd', p.astype(vp.dtype), vp)

def _stick_breaking_mixer(h, w_in, w_out):
    b, l, _ = h.shape
    qkv = (h @ w_in).reshape(b, l, 3, SB_HEADS, SB_HEAD_DIM)
    qkv = jnp.transpose(qkv, (2, 0, 3, 1, 4))
    q = qkv[0] * jnp.asarray(SB_SCALE, qkv.dtype)
    o = _block_sweep(q, qkv[1], qkv[2], _stick_breaking_block)
    return jnp.transpose(o, (0, 2, 1, 3)).reshape(b, l, SB_HEADS * SB_HEAD_DIM) @ w_out

def _rope(t, pos):
    half = t.shape[-1] // 2
    inv_freq = ROPE_THETA ** (-jnp.arange(half, dtype=jnp.float32) / half)
    ang = pos.astype(jnp.float32)[:, None] * inv_freq[None, :]
    cos = jnp.cos(ang)[None, :, None, :]
    sin = jnp.sin(ang)[None, :, None, :]
    tf = t.astype(jnp.float32)
    t1, t2 = tf[..., :half], tf[..., half:]
    return jnp.concatenate([t1 * cos - t2 * sin, t1 * sin + t2 * cos], axis=-1).astype(t.dtype)

def _mla_mixer(h, w_in, q_norm, kv_norm, w_uq, w_ukv, w_out):
    b, l, _ = h.shape
    c = h @ w_in
    c_q = c[..., :MLA_Q_RANK]
    c_kv = c[..., MLA_Q_RANK:MLA_Q_RANK + MLA_KV_RANK]
    k_rope = c[..., MLA_Q_RANK + MLA_KV_RANK:]
    pos = jnp.arange(l)
    q = (_rmsnorm(c_q, q_norm) @ w_uq).reshape(b, l, MLA_HEADS, MLA_NOPE_DIM + MLA_ROPE_DIM)
    kv = (_rmsnorm(c_kv, kv_norm) @ w_ukv).reshape(b, l, MLA_HEADS, MLA_NOPE_DIM + MLA_V_DIM)
    q = jnp.concatenate([q[..., :MLA_NOPE_DIM], _rope(q[..., MLA_NOPE_DIM:], pos)], axis=-1)
    k_rope = jnp.broadcast_to(_rope(k_rope[:, :, None, :], pos), (b, l, MLA_HEADS, MLA_ROPE_DIM))
    k = jnp.concatenate([kv[..., :MLA_NOPE_DIM], k_rope], axis=-1)
    v = kv[..., MLA_NOPE_DIM:]
    o = _block_sweep(jnp.transpose(q, (0, 2, 1, 3)), jnp.transpose(k, (0, 2, 1, 3)),
                     jnp.transpose(v, (0, 2, 1, 3)), _softmax_block)
    return jnp.transpose(o, (0, 2, 1, 3)).reshape(b, l, MLA_HEADS * MLA_V_DIM) @ w_out

def _rwkv7_scan(r, w, k, v, a, bb):
    nb, _, nh, n = r.shape

    def step(s, inp):
        r_t, w_t, k_t, v_t, a_t, b_t = inp
        sa = jnp.einsum('bhij,bhj->bhi', s, a_t)
        s = s * w_t[:, :, None, :] + sa[..., None] * b_t[:, :, None, :] + v_t[..., None] * k_t[:, :, None, :]
        return s, jnp.einsum('bhij,bhj->bhi', s, r_t)

    xs = tuple(jnp.swapaxes(t, 0, 1) for t in (r, w, k, v, a, bb))
    s0 = jnp.zeros((nb, nh, n, n), jnp.float32)
    _, y = lax.scan(step, s0, xs)
    return jnp.swapaxes(y, 0, 1)

def _rwkv7_mixer(h, mix, w_in, w0, w1, w2, a0, a1, a2, g1, g2, k_k, k_a, r_k, ln_w, ln_b, w_out):
    b, l, d = h.shape
    f32 = jnp.float32
    heads = lambda t: t.reshape(b, l, RW_HEADS, RW_HEAD_DIM)
    xx = jnp.pad(h, ((0, 0), (1, 0), (0, 0)))[:, :-1] - h
    xs = h[None] + xx[None] * mix[:, None, None, :]
    rkv = jnp.einsum('nbld,nde->nble', xs[:3], w_in)
    r, k, v = rkv[0].astype(f32), rkv[1].astype(f32), rkv[2].astype(f32)
    xw, xa, xg = xs[3], xs[4], xs[5]
    w_log = -jax.nn.softplus(-(w0 + jnp.tanh(xw @ w1) @ w2).astype(f32)) - 0.5
    decay = jnp.exp(-jnp.exp(w_log))
    a = jax.nn.sigmoid((a0 + (xa @ a1) @ a2).astype(f32))
    g = (jax.nn.sigmoid(xg @ g1) @ g2).astype(f32)
    kk = heads(k * k_k.astype(f32))
    kk = kk / jnp.maximum(jnp.linalg.norm(kk, axis=-1, keepdims=True), 1e-12)
    k = k * (1.0 + (a - 1.0) * k_a.astype(f32))
    y = _rwkv7_scan(heads(r), heads(decay), heads(k), heads(v), -kk, kk * heads(a))
    mu = jnp.mean(y, axis=-1, keepdims=True)
    var = jnp.mean(jnp.square(y - mu), axis=-1, keepdims=True)
    y = ((y - mu) * lax.rsqrt(var + RW_LN_EPS)).reshape(b, l, d) * ln_w.astype(f32) + ln_b.astype(f32)
    bonus = jnp.sum(heads(r) * heads(k) * r_k.astype(f32), axis=-1, keepdims=True) * heads(v)
    y = (y + bonus.reshape(b, l, d)) * g
    return y.astype(h.dtype) @ w_out

def setup_inputs(seed: int = 0) -> dict:
    key = jax.random.key(seed)
    counter = [0]

    def nxt():
        counter[0] += 1
        return jax.random.fold_in(key, counter[0])

    def nrm(shape, scale):
        return jax.random.normal(nxt(), shape, jnp.float32) * scale

    def gain(shape):
        return 1.0 + nrm(shape, 0.05)

    d = D_MODEL
    mla_in_w = MLA_Q_RANK + MLA_KV_RANK + MLA_ROPE_DIM
    return {
        'x': nrm((BATCH, SEQ, d), 1.0),
        'meta_tokens': nrm((N_META, d), 1.0),
        'norm_gains': gain((DEPTH, 3, 2, d)),
        'ffn_w_in': nrm((DEPTH, 2, d, 2 * D_FF), d ** -0.5),
        'ffn_w_out': nrm((DEPTH, 2, D_FF, d), D_FF ** -0.5),
        'sb_w_in': nrm((N_SB, d, 3 * SB_HEADS * SB_HEAD_DIM), d ** -0.5),
        'sb_w_out': nrm((N_SB, SB_HEADS * SB_HEAD_DIM, d), (SB_HEADS * SB_HEAD_DIM) ** -0.5),
        'mla_w_in': nrm((N_MLA, d, mla_in_w), d ** -0.5),
        'mla_q_norm': gain((N_MLA, MLA_Q_RANK)),
        'mla_kv_norm': gain((N_MLA, MLA_KV_RANK)),
        'mla_w_uq': nrm((N_MLA, MLA_Q_RANK, MLA_HEADS * (MLA_NOPE_DIM + MLA_ROPE_DIM)), MLA_Q_RANK ** -0.5),
        'mla_w_ukv': nrm((N_MLA, MLA_KV_RANK, MLA_HEADS * (MLA_NOPE_DIM + MLA_V_DIM)), MLA_KV_RANK ** -0.5),
        'mla_w_out': nrm((N_MLA, MLA_HEADS * MLA_V_DIM, d), (MLA_HEADS * MLA_V_DIM) ** -0.5),
        'rw_mix': jax.random.uniform(nxt(), (N_RWKV, 6, d), jnp.float32),
        'rw_w_in': nrm((N_RWKV, 3, d, d), d ** -0.5),
        'rw_w0': jax.random.uniform(nxt(), (N_RWKV, d), jnp.float32, -6.0, -1.0),
        'rw_w1': nrm((N_RWKV, d, RW_DECAY_LORA), d ** -0.5),
        'rw_w2': nrm((N_RWKV, RW_DECAY_LORA, d), 0.3 * RW_DECAY_LORA ** -0.5),
        'rw_a0': nrm((N_RWKV, d), 0.1),
        'rw_a1': nrm((N_RWKV, d, RW_A_LORA), d ** -0.5),
        'rw_a2': nrm((N_RWKV, RW_A_LORA, d), 0.3 * RW_A_LORA ** -0.5),
        'rw_g1': nrm((N_RWKV, d, RW_GATE_LORA), d ** -0.5),
        'rw_g2': nrm((N_RWKV, RW_GATE_LORA, d), RW_GATE_LORA ** -0.5),
        'rw_k_k': 0.85 + nrm((N_RWKV, d), 0.05),
        'rw_k_a': gain((N_RWKV, d)),
        'rw_r_k': nrm((N_RWKV, RW_HEADS, RW_HEAD_DIM), 0.1),
        'rw_ln_w': gain((N_RWKV, d)),
        'rw_ln_b': nrm((N_RWKV, d), 0.01),
        'rw_w_out': nrm((N_RWKV, d, d), d ** -0.5),
    }

def reference(x, meta_tokens, norm_gains, ffn_w_in, ffn_w_out, sb_w_in, sb_w_out,
              mla_w_in, mla_q_norm, mla_kv_norm, mla_w_uq, mla_w_ukv, mla_w_out,
              rw_mix, rw_w_in, rw_w0, rw_w1, rw_w2, rw_a0, rw_a1, rw_a2, rw_g1, rw_g2,
              rw_k_k, rw_k_a, rw_r_k, rw_ln_w, rw_ln_b, rw_w_out):
    b = x.shape[0]
    meta = jnp.broadcast_to(meta_tokens.astype(x.dtype)[None], (b, N_META, D_MODEL))
    h = jnp.concatenate([meta, x], axis=1)
    for i in range(DEPTH):
        g = norm_gains[i]
        h = h + 0.5 * _rmsnorm(_swiglu(_rmsnorm(h, g[0, 0]), ffn_w_in[i, 0], ffn_w_out[i, 0]), g[0, 1])
        u = _rmsnorm(h, g[1, 0])
        kind, slot = i % N_MIXERS, i // N_MIXERS
        if kind == 0:
            m = _stick_breaking_mixer(u, sb_w_in[slot], sb_w_out[slot])
        elif kind == 1:
            m = _mla_mixer(u, mla_w_in[slot], mla_q_norm[slot], mla_kv_norm[slot],
                           mla_w_uq[slot], mla_w_ukv[slot], mla_w_out[slot])
        else:
            m = _rwkv7_mixer(u, rw_mix[slot], rw_w_in[slot], rw_w0[slot], rw_w1[slot], rw_w2[slot],
                             rw_a0[slot], rw_a1[slot], rw_a2[slot], rw_g1[slot], rw_g2[slot],
                             rw_k_k[slot], rw_k_a[slot], rw_r_k[slot], rw_ln_w[slot], rw_ln_b[slot],
                             rw_w_out[slot])
        h = h + _rmsnorm(m, g[1, 1])
        h = h + 0.5 * _rmsnorm(_swiglu(_rmsnorm(h, g[2, 0]), ffn_w_in[i, 1], ffn_w_out[i, 1]), g[2, 1])
    return h[:, N_META:]


_drawn_inputs = setup_inputs


def setup_inputs(seed=0):
    import zlib

    import numpy as np

    out = dict(_drawn_inputs(seed))
    spreads = {}
    factors = {'rw_w1': 4.462, 'rw_w2': 4.647, 'rw_a0': 2.753, 'rw_ln_b': 8.0}
    for name, (base, spread) in spreads.items():
        noise = np.random.default_rng([zlib.crc32(name.encode()), seed]).standard_normal(out[name].shape)
        drawn = base * np.exp(spread * noise) if base else spread * noise
        out[name] = __import__('jax').numpy.asarray(drawn.astype(out[name].dtype))
    for name, factor in factors.items():
        out[name] = (out[name] * factor).astype(out[name].dtype)
    return out
```

```python
from contextlib import ExitStack

import numpy as np
import concourse.bass as bass
from concourse import mybir
from concourse.alu_op_type import AluOpType as ALU

ACT = mybir.ActivationFunctionType
AX = mybir.AxisListType
F32, F32R, BF16 = mybir.dt.float32, mybir.dt.float32r, mybir.dt.bfloat16

P = 128
D = 1024
DT_ = D // P
META, SEQ = 16, 256
L = META + SEQ
DEPTH = 4
FF = 2816
FT = FF // P
HALF = FT // 2
NH = 8
RING = 4
CAP = 11
EPS = 1e-6
LN_EPS = 64e-5
V_MIX, V_W0, V_KK, V_KA, V_RK, V_LNW, V_LNB = 5, 53, 69, 77, 85, 93, 101
LAG = 3
HSUM_AT = 6
ZP = 16
NEG = -1e30
LP = 288
CH = 32
TC = 3 * CH
GROUPS = 4
TAIL = L - P
T0, T1, T2 = slice(0, 272), slice(272, 416), slice(416, 432)
CAUSAL = 432
SB_SCALE = 1.0 / float(np.sqrt(np.float64(128)))
MLA_SCALE = 1.0 / float(np.sqrt(np.float64(192)))


class Section:

    def __init__(self, name, start, units, blocks, array, first):
        self.name, self.start, self.units, self.blocks, self.array, self.first = name, start, units, blocks, array, first
        self.iters = units // RING
        self.name_key = (name, start)


def sections(plan):
    out, at, seen = [], 0, {}
    for name, units, blocks, array in plan:
        out.append(Section(name, at, units, blocks, array, seen.get(array, 0)))
        seen[array] = seen.get(array, 0) + units
        at += units
    return out


def plan_of(layers):
    plan = []
    for layer in layers:
        kind = layer % 3
        plan += [("in", 2 * FT, DT_, "ffn_in"), ("out", 2 * DT_, HALF, "ffn_out")]
        if kind == 0:
            plan += [("q", 8, 8, "sb_in"), ("kv", 16, 8, "sb_in"), ("proj", 8, 8, "sb_out")]
        elif kind == 1:
            plan += [("mla_in", 8, 6, "mla_in"), ("mla_uq", 4, 9, "mla_uq"), ("mla_ukv", 4, 8, "mla_ukv"),
                     ("proj", 8, 8, "mla_out")]
        else:
            plan += [("r", 8, 8, "rw_in"), ("k", 8, 8, "rw_in"), ("v", 8, 8, "rw_in"), ("lora1", 4, 8, "rw_lora1"), ("lora2", 4, 8, "rw_lora2"),
                     ("proj", 8, 8, "rw_out")]
        plan += [("in", 2 * FT, DT_, "ffn_in"), ("out", 2 * DT_, HALF, "ffn_out")]
    return plan


class Steps:

    def __init__(self, eng, sem):
        self.eng, self.sem, self.n = eng, sem, 0

    def link(self, ins):
        ins.then_inc(self.sem, 1)
        self.n += 1
        self.eng.wait_ge(self.sem, self.n)


def build(nc, A, out, layers):
    secs = sections(plan_of(layers))
    ctx = ExitStack()
    with ctx:
        sb = lambda name, shape, dt=F32: ctx.enter_context(nc.sbuf_tensor(name, shape, dt))
        sem = lambda name: ctx.enter_context(nc.semaphore(name))

        h = sb("h", [P, DT_, L])
        x_hi, x_lo = sb("x_hi", [P, DT_, L], F32R), sb("x_lo", [P, DT_, L], F32R)
        m = sb("m", [P, DT_, L])
        raw = sb("raw", [P, RING, CAP * P])
        w_hi, w_lo = sb("w_hi", [P, RING, CAP * P], F32R), sb("w_lo", [P, RING, CAP * P], F32R)
        sq = sb("sq", [P, 2, L])
        xm = sb("xm", [P, 2, L])
        pend, pad1 = sb("pend", [P, DT_, 8]), sb("pad1", [P, 1])
        acc, std, rstd = sb("acc", [P, L]), sb("std", [P, L]), sb("rstd", [P, L])
        xr = xm[:, 0, :]
        gains = sb("gains", [P, DEPTH * 6 * DT_])
        NC = A["consts"].shape[1]
        consts = sb("consts", [P, NC])
        bc = lambda cols, width: cols.unsqueeze(2).broadcast_to([P, cols.shape[1], width])
        cbf = sb("cbf", [P, 4 * P + 16], BF16)
        ident, ones = consts[:, 0:P], consts[:, P:2 * P]
        ntri, nones = consts[:, 2 * P:3 * P], consts[:, 3 * P:4 * P]
        eps_col, eps4_col, one_col = (consts[:, 7 * P + 16 + k:7 * P + 17 + k] for k in range(3))
        ln_eps_col = consts[:, 7 * P + 19:7 * P + 20]
        C0 = 7 * P + 24
        cos2, sin2 = consts[:, C0:C0 + L], consts[:, C0 + L:C0 + 2 * L]
        rot = consts[:, C0 + 2 * L:C0 + 2 * L + P]
        vecs = sb("vecs", [P, A["vecs"].shape[1]])

        bank = [ctx.enter_context(nc.psum_tensor(f"bank{b}", [P, 512], F32)) for b in range(8)]

        with ExitStack() as place:
            ps = lambda name, shape, dt=F32: place.enter_context(nc.sbuf_tensor(name, shape, dt))
            hid_hi, hid_lo = ps("hid_hi", [P, FT, L], F32R), ps("hid_lo", [P, FT, L], F32R)
            gs, up, sg, hid = (ps(n, [P, 2, L]) for n in ("gs", "up", "sg", "hid"))
        with ExitStack() as place:
            ps = lambda name, shape, dt=F32: place.enter_context(nc.sbuf_tensor(name, shape, dt))
            qkv = ps("qkv", [P, 24, L])
            vt = ps("vt", [P, 3, D])
            zraw, zneg, zexp, zln, zsp, prob = (ps(n, [P, 2, CAUSAL]) for n in ("zraw", "zneg", "zexp", "zln", "zsp", "prob"))
        with ExitStack() as place:
            ps = lambda name, shape, dt=F32: place.enter_context(nc.sbuf_tensor(name, shape, dt))
            lat = ps("lat", [P, 6, L])
            mq, mk, mv = ps("mq", [P, NH, L]), ps("mk", [P, NH, L]), ps("mv", [P, NH, L])
            qz = ps("qz", [P, NH, L])
            qr = ps("qr", [P, NH // 2, L])
            kr = ps("kr", [P, L])
            rtmp = ps("rtmp", [P, 2, L])
            mvt = ps("mvt", [P, 3, D])
            pa, pb = ps("pa", [P, 2, 384]), ps("pb", [P, 2, 384])
            top, ntop, tot, rtot = (ps(n, [P, 2, 3]) for n in ("top", "ntop", "tot", "rtot"))
            pT = ps("pT", [P, 2, CAUSAL])

        ident_bf, causal_bf, causal_tail_bf, strict_bf = (cbf[:, P * k:P * (k + 1)] for k in range(4))
        strict_tail_bf = cbf[:, 4 * P:4 * P + 16]

        with ExitStack() as place:
            ps = lambda name, shape, dt=F32: place.enter_context(nc.sbuf_tensor(name, shape, dt))
            r_, k_, w_, a_, v_ = (ps(n, [P, DT_, LP]) for n in ("r_", "k_", "w_", "a_", "v_"))
            g_ = ps("g_", [P, DT_, L])
            rwc = ps("rwc", [P, A["rwc"].shape[1]])
            with ExitStack() as place2:
                ps = lambda name, shape, dt=F32: place2.enter_context(nc.sbuf_tensor(name, shape, dt))
                xx, lt = ps("xx", [P, DT_, L]), ps("lt", [P, 4, L])
                lr_hi, lr_lo = ps("lr_hi", [P, 4, L], F32R), ps("lr_lo", [P, 4, L], F32R)
            with ExitStack() as place2:
                ps = lambda name, shape, dt=F32: place2.enter_context(nc.sbuf_tensor(name, shape, dt))
                cs, ex, ex2 = (ps(n, [P, DT_, L]) for n in ("cs", "ex", "ex2"))
            with ExitStack() as place2:
                ps = lambda name, shape, dt=F32: place2.enter_context(nc.sbuf_tensor(name, shape, dt))
                tok = ps("tok", [TC, 3, 3, 256])
                inv = ps("inv", [TC, 4, LP])
                rb = ps("rb", [TC, 4, LP])
                akv = ps("akv", [TC, 3, 256])
                with ExitStack() as place3:
                    ps = lambda name, shape, dt=F32: place3.enter_context(nc.sbuf_tensor(name, shape, dt))
                    am, aml, tinv, yl = (ps(n, [TC, 2, LP]) for n in ("am", "aml", "tinv", "yl"))
                    ak, rk = ps("ak", [TC, LP]), ps("rk", [TC, LP])
                with ExitStack() as place3:
                    ps = lambda name, shape, dt=F32: place3.enter_context(nc.sbuf_tensor(name, shape, dt))
                    u_, sa = ps("u_", [TC, 256]), ps("sa", [TC, 3, 256])
                    state, spre, gate, upd = (ps(n, [P, 256]) for n in ("state", "spre", "gate", "upd"))
            with ExitStack() as place2:
                ps = lambda name, shape, dt=F32: place2.enter_context(nc.sbuf_tensor(name, shape, dt))
                yc, ysq, ystd, yrs, yn, yg = (ps(n, [P, 2, L]) for n in ("yc", "ysq", "ystd", "yrs", "yn", "yg"))
        bones = rwc[:, 0:P]
        m_lower, m_upper, m_upper_eq = (rwc[0:TC, P + TC * k:P + TC * k + TC] for k in range(3))
        m_level = [rwc[0:TC, P + TC * (3 + k):P + TC * (4 + k)] for k in range(5)]
        pair_mask = rwc[:, P + 8 * TC:2 * P + 8 * TC]
        restart = rwc[:, 2 * P + 8 * TC:2 * P + 8 * TC + L]
        tri3 = lambda mk: mk.unsqueeze(1).broadcast_to([TC, 3, TC])
        t3 = lambda ap: ap.rearrange("p (t c) -> p t c", t=3)

        group_items = []
        for T in range(3):
            group_items += [("tok", T, 0), ("tok", T, 1)]
        for pr in range(2):
            for e in range(2):
                group_items += [(x, pr, e) for x in ("A", "Ak", "Rb", "Rk")] + [("akv", pr, e)]
            group_items += [("X", pr, e) for e in range(2)]
            for lv in range(1, 5):
                group_items += [("Y", pr, lv, e) for e in range(2)]
                group_items += [(x, pr, lv, e) for e in range(2) for x in (("Z", "ZT") if lv < 4 else ("Z",))]
        rolling = {key: 2 + at % 6 for at, key in enumerate(group_items)}

        loaded = sem("loaded")
        raw_arrived = [sem(f"raw_arrived{s}") for s in range(RING)]
        hi_ready, lo_ready = sem("hi_ready"), sem("lo_ready")
        unit_used = sem("unit_used")
        bank_free = [sem(f"bank_free{b}") for b in range(8)]
        sg_ready, hid_made, hhi_made, hid_ready = sem("sg_ready"), sem("hid_made"), sem("hhi_made"), sem("hid_ready")
        hg_hi_ready, hsq_ready, hacc_ready, hsum_done = (sem(n) for n in ("hg_hi_ready", "hsq_ready", "hacc_ready", "hsum_done"))
        sq_ready, sq_free = sem("sq_ready"), sem("sq_free")
        sum_done, std_ready = sem("sum_done"), sem("std_ready")
        apply_ready, h_ready = sem("apply_ready"), sem("h_ready")
        xf_ready, xhi_ready, x_ready = sem("xf_ready"), sem("xhi_ready"), sem("x_ready")
        kkraw_ready, tile_done = sem("kkraw_ready"), sem("tile_done")
        cbf_ready = sem("cbf_ready")
        act_tile, dve_tile = sem("act_tile"), sem("dve_tile")
        z_ready, zraw_ready, zneg_ready, zexp_ready, zln_ready = sem("z_ready"), sem("zraw_ready"), sem("zneg_ready"), sem("zexp_ready"), sem("zln_ready")
        zsp_ready, r_ready, prob_ready = sem("zsp_ready"), sem("r_ready"), sem("prob_ready")
        o_ready, ohi_ready = sem("o_ready"), sem("ohi_ready")
        vt_done = sem("vt_done")
        rot_ready, rope_ready = sem("rot_ready"), sem("rope_ready")
        zq_ready, ntop_ready, exp_ready, p_ready, pT_done = (sem(n) for n in ("zq_ready", "ntop_ready", "exp_ready", "p_ready", "pT_done"))
        xm_ready, lt_ready, lhi_ready = sem("xm_ready"), sem("lt_ready"), sem("lhi_ready")
        rwc_loaded, sig_ready = sem("rwc_loaded"), sem("sig_ready")
        kksq_ready, kkmax_ready, kkroot_ready, head_sum = (sem(n) for n in ("kksq_ready", "kkmax_ready", "kkroot_ready", "head_sum"))
        cs_ready, csprev_ready, pprev_ready, pinv_ready, pinc_ready = (sem(n) for n in ("cs_ready", "csprev_ready", "pprev_ready", "pinv_ready", "pinc_ready"))
        bonus_ready, ops_ready = sem("bonus_ready"), sem("ops_ready")
        tok_done, gram_done, akv_done, y_done, z_done = (sem(n) for n in ("tok_done", "gram_done", "akv_done", "y_done", "z_done"))
        am_ready, aml_ready = sem("am_ready"), sem("aml_ready")
        u_done, u_ready, sa_done, sa_ready, s_done = (sem(n) for n in ("u_done", "u_ready", "sa_done", "sa_ready", "s_done"))
        spre_ready, state_ready, out_done = sem("spre_ready"), sem("state_ready"), sem("out_done")
        mean_done, yc_ready, ysq_ready, var_done, ystd_ready, yg_ready = (sem(n) for n in ("mean_done", "yc_ready", "ysq_ready", "var_done", "ystd_ready", "yg_ready"))
        dve_chain, act_chain, pool_chain = sem("dve_chain"), sem("act_chain"), sem("pool_chain")
        stored = sem("stored")
        block = ctx.enter_context(nc.Block())

        def rounds(eng, sec, body, ahead, peel=False):
            if peel:
                body(0, lambda s: ahead(sec, 1, s))
            if sec.iters > 1 + peel:
                with eng.Fori(1 if peel else 0, sec.iters - 1) as i:
                    body(i, lambda s: ahead(sec, i + 1, s))
            after = following[sec.name_key]
            body(sec.iters - 1, lambda s: ahead(after, 0, s) if after else None)

        z_banks = (4, 5, 0, 1)
        following = {s.name_key: t for s, t in zip(secs, secs[1:] + [None])}

        def gain(layer, sub, post, j):
            c = ((layer * 3 + sub) * 2 + post) * DT_ + j
            return gains[:, c:c + 1]

        uses_at = {}

        @block.tensor
        def _(pe):
            uses = [0] * 8
            n = dict(x=0, hid=0, sq=0, head=0, mhead=0, vt=0, hsum=0)
            take = iter(secs)

            def claim(b):
                pe.wait_ge(bank_free[b], uses[b] + 1)
                uses[b] += 1

            def taken(*banks):
                for b in banks:
                    pe.wait_ge(bank_free[b], uses[b] + 1)

            def product(sec, block_of, ready, only=None, each_tile=False, first=None):
                if not only:
                    uses_at[sec.name_key] = list(uses)
                firsts = {}
                for s in range(RING):
                    for j in range(sec.blocks):
                        b, k, (xh, xl), start, stop = block_of(s, j)
                        if start:
                            firsts[b] = firsts.get(b, 0) + 1

                def body(i, ahead):
                    seen = {}
                    for s in range(RING):
                        pe.wait_ge(lo_ready, sec.start + RING * i + s + 1)
                        for j in range(sec.blocks):
                            b, k, (xh, xl), start, stop = block_of(s, j)
                            if start:
                                pe.wait_ge(bank_free[b], uses[b] + firsts[b] * i + seen.get(b, 0) + 1)
                                seen[b] = seen.get(b, 0) + 1
                            ready(s, k)
                            o, wh, wl = bank[b][:, 0:L], w_hi[:, s, P * j:P * j + P], w_lo[:, s, P * j:P * j + P]
                            nc.tensor.matmul(o, wh, xh[:, k, :], start=start, stop=False)
                            nc.tensor.matmul(o, wh, xl[:, k, :], start=False, stop=False)
                            last = nc.tensor.matmul(o, wl, xh[:, k, :], start=False, stop=stop)
                            if each_tile and stop and j + 1 < sec.blocks:
                                last.then_inc(tile_done, 1)
                        last.then_inc(unit_used, 1)
                if only is not None:
                    base = list(uses)
                    for b, c in firsts.items():
                        uses[b] = base[b] - c * only
                    body(only, None)
                    for b, c in firsts.items():
                        uses[b] = base[b] + c
                    return
                if first:
                    first(sec)
                rounds_plain(pe, sec, body, 1 if first else 0)
                for b, c in firsts.items():
                    uses[b] += c * sec.iters

            def rounds_plain(eng, sec, body, start=0):
                if sec.iters > 1 + start:
                    with eng.Fori(start, sec.iters) as i:
                        body(i, None)
                else:
                    body(start, None)

            x_parts, hid_parts = (x_hi, x_lo), (hid_hi, hid_lo)

            def x_ready_first(count=DT_, last_slot=0):
                base = n["x"]
                n["x"] += count
                return lambda s, k: pe.wait_ge(x_ready, base + k + 1) if s <= last_slot else None

            def input_sum():
                n["hsum"] += 1
                pe.wait_ge(hacc_ready, n["hsum"])
                nc.tensor.matmul(bank[5][:, 0:L], ones, acc[:, :], start=True, stop=True).then_inc(hsum_done, 1)

            def first_round(sec):
                base = n["x"]
                n["x"] += DT_
                for pair in ((0, 1), (2, 3)):
                    for s in pair:
                        pe.wait_ge(lo_ready, sec.start + s + 1)
                        pe.wait_ge(bank_free[s], uses[s] + 1)
                    for k in range(DT_):
                        if pair[0] == 0:
                            pe.wait_ge(x_ready, base + k + 1)
                        elif k == HSUM_AT:
                            input_sum()
                        for s in pair:
                            o, wh, wl = bank[s][:, 0:L], w_hi[:, s, P * k:P * k + P], w_lo[:, s, P * k:P * k + P]
                            nc.tensor.matmul(o, wh, x_hi[:, k, :], start=(k == 0), stop=False)
                            nc.tensor.matmul(o, wh, x_lo[:, k, :], start=False, stop=False)
                            last = nc.tensor.matmul(o, wl, x_hi[:, k, :], start=False, stop=(k == DT_ - 1))
                            if k == DT_ - 1:
                                last.then_inc(unit_used, 1)

            def whole(s, j):
                return s, j, x_parts, j == 0, j == 7

            def halves(s, j):
                k = HALF * (s % 2) + j
                return 2 * (s // 2), k, hid_parts, k == 0, k == FT - 1

            def sum_squares(count, b):
                for k in range(count):
                    pe.wait_ge(sq_ready, n["sq"] + 1)
                    nc.tensor.matmul(bank[b][:, 0:L], ones, sq[:, n["sq"] % 2, :], start=(k == 0),
                                     stop=(k == count - 1)).then_inc(sq_free, 1)
                    n["sq"] += 1

            def sum_output():
                n["sq"] += DT_
                pe.wait_ge(sq_free, 2 + n["sq"])
                nc.tensor.matmul(bank[4][:, 0:L], ones, acc[:, :], start=True, stop=True).then_inc(sum_done, 1)

            def swiglu():
                product(next(take), whole, lambda s, k: None, first=first_round)
                base = n["hid"]
                n["hid"] += FT
                product(next(take), halves, lambda s, k: pe.wait_ge(hid_ready, 2 + base + k + 1) if s < 2 else None)
                sum_output()

            def token_major(src, dst_tokens=(0, P, TAIL)):
                g = 0
                for t0 in dst_tokens:
                    for four in range(2):
                        b = 4 + g % 4
                        claim(b)
                        for q in range(4):
                            last = nc.tensor.transpose(bank[b][:, P * q:P * q + P], src(4 * four + q)[:, t0:t0 + P], ident)
                        last.then_inc(vt_done, 1)
                        g += 1

            def head_output(v, w, b):
                claim(b)
                o = bank[b]
                nc.tensor.matmul(o[:, 0:L], v(0), w[:, T0], start=True, stop=False)
                nc.tensor.matmul(o[:, P:L], v(1), w[:, T1], start=False, stop=False)
                nc.tensor.matmul(o[:, 2 * P:L], v(2), w[:, T2], start=False, stop=True).then_inc(o_ready, 1)
                n["head"] += 1

            def stick_breaking():
                product(next(take), whole, lambda s, k: None, first=first_round)
                product(next(take), whole, lambda s, k: None)
                taken(0, 1, 2, 3)
                token_major(lambda hd: qkv[:, 16 + hd, :])
                base = n["mhead"]

                def scores(hd):
                    b = z_banks[hd % 4]
                    claim(b)
                    z, q, k = bank[b], qkv[:, hd, :], qkv[:, 8 + hd, :]
                    nc.tensor.matmul(z[:, 0:272], k[:, 0:P], q[:, 0:L], start=True, stop=False)
                    nc.tensor.matmul(z[:, 272:416], k[:, P:2 * P], q[:, P:L], start=False, stop=False)
                    nc.tensor.matmul(z[:, 416:432], k[:, TAIL:L], q[:, 2 * P:L], start=False, stop=False)
                    nc.tensor.matmul(z[:, 0:128], ident_bf, strict_bf, start=False, stop=False)
                    nc.tensor.matmul(z[:, 272:400], ident_bf, strict_bf, start=False, stop=False)
                    nc.tensor.matmul(z[:, 416:432], ident_bf, strict_tail_bf, start=False, stop=True).then_inc(z_ready, 1)

                def suffix_sums(hd):
                    z, y = bank[z_banks[hd % 4]], zsp[:, hd % 2, :]
                    pe.wait_ge(zsp_ready, base + hd + 1)
                    for k, (cols, w, src) in enumerate((((0, 272), ntri, (0, 272)), ((128, 272), nones, (272, 416)),
                                                        ((256, 272), nones, (416, 432)), ((272, 416), ntri, (272, 416)),
                                                        ((400, 416), nones, (416, 432)), ((416, 432), ntri, (416, 432)))):
                        last = nc.tensor.matmul(z[:, cols[0]:cols[1]], w, y[:, src[0]:src[1]], start=False, stop=(k == 5),
                                                skip_group_check=True)
                    last.then_inc(r_ready, 1)

                pe.wait_ge(cbf_ready, 1)
                taken(4, 5, 6, 7)
                scores(0)
                scores(1)
                for hd in range(NH + 1):
                    if hd + 2 < NH:
                        scores(hd + 2)
                    if hd < NH:
                        suffix_sums(hd)
                    if hd >= 1:
                        g = hd - 1
                        taken(z_banks[g % 4])
                        head_output(lambda t: vt[:, t, P * g:P * g + P], prob[:, g % 2, :], 6 + g % 2)
                n["mhead"] += NH
                taken(6, 7)
                product(next(take), whole, lambda s, k: None)
                sum_output()

            def latent_attention():
                def in_round(i):
                    def thirds(s, j):
                        g = 24 * i + 6 * s + j
                        return (g // 8) % 4, g % 8, x_parts, g % 8 == 0, g % 8 == 7
                    return thirds

                sec, ready = next(take), x_ready_first(last_slot=1)
                uses_at["latents"] = list(uses)

                def ready_or_sum(s, k):
                    if (s, k) == (3, 2):
                        input_sum()
                    ready(s, k)

                for i in range(2):
                    product(sec, in_round(i), ready_or_sum if i == 0 else lambda s, k: None, only=i)
                sum_squares(3, 5)
                sum_squares(2, 4)
                base = n["x"]
                n["x"] += 5

                def of_query(s, j):
                    t, k = 3 * s + j // 3, j % 3
                    return t % 4, k, x_parts, k == 0, k == 2

                def of_key(s, j):
                    t, k = 4 * s + j // 2, j % 2
                    return t % 4, 3 + k, x_parts, k == 0, k == 1

                product(next(take), of_query, lambda s, k: pe.wait_ge(x_ready, base + k + 1) if s == 0 else None)
                product(next(take), of_key, lambda s, k: pe.wait_ge(x_ready, base + k + 1) if s == 0 else None)
                taken(0, 1, 2, 3)
                uses_at["rope"] = list(uses)
                for t in range(5):
                    claim(4 + t % 4)
                    nc.tensor.matmul(bank[4 + t % 4][:, 0:L], rot, qr[:, t, :] if t < 4 else lat[:, 5, :], start=True,
                                     stop=True).then_inc(rot_ready, 1)
                token_major(lambda hd: mv[:, hd, :])
                taken(4, 5, 6, 7)
                pe.wait_ge(cbf_ready, 1)

                def scores(hd):
                    a, c = 4 + hd % 2, 6 + hd % 2
                    claim(a)
                    claim(c)
                    za, zc = bank[a], bank[c]
                    parts = ((za[:, 0:128], 0, slice(0, P), causal_bf, za[:, 0:128]),
                             (za[:, 128:384], P, slice(0, 2 * P), causal_bf, za[:, 256:384]),
                             (zc[:, 0:256], TAIL, slice(0, 2 * P), None, None),
                             (zc[:, 256:384], TAIL, slice(TAIL, L), causal_tail_bf, zc[:, 256:384]))
                    for g, (o, q0, keys, mask, where) in enumerate(parts):
                        nc.tensor.matmul(o, mq[:, hd, q0:q0 + P], mk[:, hd, keys], start=g in (0, 2), stop=False)
                        last = nc.tensor.matmul(o, qz[:, hd, q0:q0 + P], kr[:, keys], start=False, stop=mask is None and False)
                        if mask is not None:
                            last = nc.tensor.matmul(where, ident_bf, mask, start=False, stop=g in (1, 3))
                    last.then_inc(zq_ready, 1)

                def transposed(hd):
                    z = hd % 2
                    pe.wait_ge(p_ready, hd + 1)
                    claim(z)
                    o = bank[z]
                    for at, src in ((0, pa[:, z, 0:128]), (128, pa[:, z, 128:256]), (272, pa[:, z, 256:384])):
                        nc.tensor.transpose(o[:, at:at + P], src, ident)
                    for at, k0 in ((256, 0), (400, 128), (416, 256)):
                        last = nc.tensor.matmul(o[:, at:at + 16], pb[:, z, k0:k0 + P], ident[:, 112:128], start=True, stop=True)
                    last.then_inc(pT_done, 1)

                scores(0)
                scores(1)
                for hd in range(NH):
                    transposed(hd)
                    if hd + 2 < NH:
                        scores(hd + 2)
                    pe.wait_ge(bank_free[hd % 2], uses[hd % 2] + 1)
                    head_output(lambda t: mvt[:, t, P * hd:P * hd + P], pT[:, hd % 2, :], 2 + hd % 2)
                taken(2, 3)
                product(next(take), whole, lambda s, k: None)
                sum_output()

            def time_mixing():
                for name in "rkv":
                    product(next(take), whole, x_ready_first())
                base = n["x"]
                n["x"] += 3 * DT_
                product(next(take), whole, lambda s, k: pe.wait_ge(x_ready, base + DT_ * min(s, 2) + k + 1) if s < 3 else None)
                taken(0, 1, 2, 3)
                lr = (lr_hi, lr_lo)

                def second(s, j):
                    if s < 2:
                        return j % 4, s, lr, True, True
                    return (4 * (s % 2) + j // 2) % 4, 2 + j % 2, lr, j % 2 == 0, j % 2 == 1

                product(next(take), second, lambda s, k: None, each_tile=True)
                pe.wait_ge(rwc_loaded, 16)
                uses_at["kk"] = list(uses)
                for what in (kksq_ready, bonus_ready):
                    pe.wait_ge(what, 1)
                    src = ex
                    for k in range(DT_):
                        claim(k)
                        nc.tensor.matmul(bank[k][:, 0:L], bones, src[:, k, :], start=True, stop=True).then_inc(head_sum, 1)
                pe.wait_ge(ops_ready, 1)
                for grp in range(GROUPS):
                    group(grp)
                uses_at["ln"] = list(uses)
                for k in range(DT_):
                    claim(k % 2)
                    nc.tensor.matmul(bank[k % 2][:, 0:L], bones, v_[:, k, 0:L], start=True, stop=True).then_inc(mean_done, 1)
                    claim(2 + k % 2)
                    pe.wait_ge(ysq_ready, k + 1)
                    nc.tensor.matmul(bank[2 + k % 2][:, 0:L], bones, ysq[:, k % 2, :], start=True, stop=True).then_inc(var_done, 1)
                base = n["x"]
                n["x"] += DT_
                product(next(take), whole, lambda s, k: pe.wait_ge(x_ready, base + k + 1) if s == 0 else None)
                sum_output()

            def group(grp):
                tiles = (2 * grp, 2 * grp + 1)

                def roll(*key):
                    claim(rolling[key])
                    return bank[rolling[key]]

                for T in range(3):
                    for half, srcs in enumerate(((a_, k_), (v_,))):
                        o = roll("tok", T, half)
                        for x, src in enumerate(srcs):
                            for pp in range(2):
                                last = nc.tensor.transpose(o[0:TC, 256 * x + P * pp:256 * x + P * pp + P],
                                                           src[:, tiles[pp], TC * T:TC * T + TC], ident)
                        last.then_inc(tok_done, 1)
                for pr in range(2):
                    j = tiles[pr]
                    for e in range(2):
                        f = slice(64 * e, 64 * e + 64)
                        for x, (left, right) in (("A", (w_, a_)), ("Ak", (k_, w_)), ("Rb", (a_, r_)), ("Rk", (k_, r_))):
                            o = roll(x, pr, e)
                            for T in range(3):
                                c = slice(TC * T, TC * T + TC)
                                last = nc.tensor.matmul(o[0:TC, c], left[f, j, c], right[f, j, c], start=(T == 0), stop=(T == 2))
                            last.then_inc(gram_done, 1)
                        q = 2 * pr + e
                        vcol = slice(64 * q, 64 * q + 64)
                        pe.wait_ge(bank_free[rolling["Ak", pr, e]], uses[rolling["Ak", pr, e]] + 1)
                        o = roll("akv", pr, e)
                        for T in range(3):
                            last = nc.tensor.matmul(o[0:TC, 64 * T:64 * T + 64], ak[:, TC * T:TC * T + TC], tok[:, T, 2, vcol],
                                                    start=(T == 0), stop=(T == 2))
                        last.then_inc(akv_done, 1)
                        pe.wait_ge(bank_free[rolling["Rk", pr, e]], uses[rolling["Rk", pr, e]] + 1)
                        if e == 0:
                            claim(pr)
                        for T in range(3):
                            c = slice(TC * T, TC * T + TC)
                            last = nc.tensor.matmul(bank[pr][64 * e:64 * e + 64, c], tok[:, T, 2, vcol], rk[:, c], start=(T == 0),
                                                    stop=(T == 2))
                        last.then_inc(akv_done, 1)
                    for e in range(2):
                        taken(rolling["A", pr, e])
                        o = roll("X", pr, e)
                        for T in range(3):
                            c = slice(TC * T, TC * T + TC)
                            last = nc.tensor.transpose(o[0:TC, c], tinv[:, e, c], ident[0:TC, 0:TC])
                        last.then_inc(z_done, 1)
                    for lv in range(1, 5):
                        for e in range(2):
                            q = 2 * pr + e
                            before = ("X", pr, e) if lv == 1 else ("Z", pr, lv - 1, e)
                            for b in {rolling[before]} | ({rolling["ZT", pr, lv - 1, e]} if lv > 1 else set()):
                                pe.wait_ge(bank_free[b], uses[b] + 1)
                            pe.wait_ge(aml_ready, 4 * (4 * grp + 2 * pr) + 2 * (lv - 1) + e + 1)
                            o = roll("Y", pr, lv, e)
                            for T in range(3):
                                c = slice(TC * T, TC * T + TC)
                                last = nc.tensor.matmul(o[0:TC, c], aml[:, e, c], inv[:, q, c], start=(T == 0), stop=(T == 2))
                            last.then_inc(y_done, 1)
                        for e in range(2):
                            q = 2 * pr + e
                            b = rolling["Y", pr, lv, e]
                            pe.wait_ge(bank_free[b], uses[b] + 1)
                            for x, (left, right) in (("Z", (tinv, yl)), ("ZT", (yl, tinv)))[:2 if lv < 4 else 1]:
                                o = roll(x, pr, lv, e)
                                for T in range(3):
                                    c = slice(TC * T, TC * T + TC)
                                    last = nc.tensor.matmul(o[0:TC, c], left[:, e, c], right[:, e, c], start=(T == 0), stop=(T == 2))
                                last.then_inc(z_done, 1)
                pe.wait_ge(bank_free[rolling["Z", 1, 4, 0]], uses[rolling["Z", 1, 4, 0]] + 1)
                taken(2, 3, 4, 5, 6, 7)
                for c in range(9):
                    T, base, count = c // 3, CH * (c % 3), 9 * grp + c
                    rows, toks = slice(base, base + CH), slice(CH * c, CH * c + CH)
                    pe.wait_ge(state_ready, count + 1)
                    for pp in range(2):
                        last = nc.tensor.matmul(bank[2][rows, P * pp:P * pp + P], w_[:, tiles[pp], toks], state[:, P * pp:P * pp + P],
                                                start=(pp == 0), stop=(pp == 1))
                    last.then_inc(u_done, 1)
                    for pp in range(2):
                        nc.tensor.matmul(bank[pp][:, toks], state[:, P * pp:P * pp + P], r_[:, tiles[pp], toks], start=False, stop=False,
                                         skip_group_check=True)
                    pe.wait_ge(u_ready, count + 1)
                    for q in range(4):
                        last = nc.tensor.matmul(bank[3][rows, 64 * q:64 * q + 64], inv[:, q, TC * T + base:TC * T + base + CH],
                                                u_[:, 64 * q:64 * q + 64], start=(q == 0), stop=(q == 3))
                    last.then_inc(sa_done, 1)
                    pe.wait_ge(sa_ready, count + 1)
                    if c < 8:
                        for pp in range(2):
                            col = slice(P * pp, P * pp + P)
                            nc.tensor.matmul(bank[4][:, col], tok[rows, T, 0, col], sa[rows, T, col], start=(pp == 0), stop=False)
                            last = nc.tensor.matmul(bank[4][:, col], tok[rows, T, 1, col], tok[rows, T, 2, col], start=False, stop=(pp == 1))
                        last.then_inc(s_done, 1)
                for pp in range(2):
                    for e in range(2):
                        q = 2 * pp + e
                        for T in range(3):
                            c = slice(TC * T, TC * T + TC)
                            last = nc.tensor.matmul(bank[pp][64 * e:64 * e + 64, c], sa[:, T, 64 * q:64 * q + 64], rb[:, q, c],
                                                    start=False, stop=(e == 1 and T == 2), skip_group_check=True)
                    last.then_inc(out_done, 1)

            pe.wait_ge(loaded, 64)
            for at, layer in enumerate(layers):
                swiglu()
                if layer % 3 == 2:
                    sum_squares(DT_, 5)
                (stick_breaking, latent_attention, time_mixing)[layer % 3]()
                swiglu()

        @block.sync
        def _(sp):
            for b in range(8):
                sp.sem_inc(bank_free[b], 1)
            sp.sem_inc(sq_free, 2)
            sp.sem_inc(hid_ready, 2)
            sp.dma_start(h[:, :, :], A["h0"]).then_inc(loaded, 16)

            def load(sec, i, s, first=False):
                u = sec.start + RING * i + s
                if not first:
                    sp.wait_ge(lo_ready, u - RING + 1)
                sp.dma_start(raw[:, s, 0:sec.blocks * P],
                             A[sec.array][sec.first + RING * i + s, :, :]).then_inc(raw_arrived[s], 16)

            for s in range(RING):
                load(secs[0], 0, s, first=True)
            sp.dma_start(gains[:, :], A["gains"]).then_inc(loaded, 16)
            sp.dma_start(consts[:, :], A["consts"]).then_inc(loaded, 16)
            sp.dma_start(vecs[:, :], A["vecs"]).then_inc(loaded, 16)
            for sec in secs:
                start = 1 if sec.start == 0 else 0
                if sec.iters - start > 1:
                    with sp.Fori(start, sec.iters) as i:
                        for s in range(RING):
                            load(sec, i, s)
                elif sec.iters > start:
                    for s in range(RING):
                        load(sec, start, s)
                if sec.name == "r":
                    sp.wait_ge(unit_used, sec.start)
                    sp.dma_start(rwc[:, :], A["rwc"]).then_inc(rwc_loaded, 16)
            sp.wait_ge(h_ready, DT_ * 3 * len(layers))
            sp.dma_start(out, h[:, :, META:L]).then_inc(stored, 16)
            sp.wait_ge(stored, 16)

        
        @block.scalar
        def _(act):
            steps = Steps(act, act_chain)
            n = dict(sq=0, sg=0, norm=0, xf=0, h=0, hid=0, head=0, mhead=0, vt=0, hsum=0)
            take = iter(secs)

            def split_hi(sec, i, s, first=False):
                u = sec.start + RING * i + s
                act.wait_ge(raw_arrived[s], 16 * (sec.start // RING + i + 1))
                if not first:
                    act.wait_ge(unit_used, u - RING + 1)
                nc.scalar.activation(w_hi[:, s, 0:sec.blocks * P], raw[:, s, 0:sec.blocks * P],
                                     ACT.Copy).then_inc(hi_ready, 1)

            def square(src, k, at):
                act.wait_ge(sq_free, at + 1)
                nc.scalar.activation(sq[:, k % 2, :], src, ACT.Square).then_inc(sq_ready, 1)

            def root(b, width, doubled=False):
                nc.scalar.activation(std[:, :], bank[b][:, 0:L], ACT.Sqrt, bias=eps4_col if doubled else eps_col,
                                     scale=(4.0 if doubled else 1.0) / width).then_inc(std_ready, 1)

            def norm_in(tiles, width, wait_tile, parts=True):
                for k, src in enumerate(tiles):
                    wait_tile(k)
                    square(src, n["sq"] + k, n["sq"] + k)
                n["sq"] += len(tiles)
                finish_norm(len(tiles), width, n["sq"], parts=parts)

            def finish_norm(count, width, squares, k0=0, b=5, parts=True):
                act.wait_ge(sq_free, 2 + squares)
                root(b, width)
                if not parts:
                    n["xf"] += count
                    return
                for k in range(k0, k0 + count):
                    n["xf"] += 1
                    act.wait_ge(xf_ready, n["xf"])
                    nc.scalar.activation(x_hi[:, k, :], m[:, k, :], ACT.Copy).then_inc(xhi_ready, 1)

            def residual_norm_in():
                n["h"] += DT_
                norm_in([h[:, k, :] for k in range(DT_)], D, lambda k: act.wait_ge(h_ready, n["h"] - DT_ + k + 1), False)

            def gained(layer, sub, first=False):
                for k in range(DT_):
                    if not first:
                        n["h"] += 1
                        act.wait_ge(h_ready, n["h"])
                    nc.scalar.activation(x_hi[:, k, :], h[:, k, :], ACT.Copy, scale=gain(layer, sub, 0, k)).then_inc(hg_hi_ready, 1)
                nc.scalar.activation(m[:, :, :], h[:, :, :], ACT.Square).then_inc(hsq_ready, 1)

            def input_root():
                n["hsum"] += 1
                act.wait_ge(hsum_done, n["hsum"])
                root(5, D)

            def norm_out(half):
                n["norm"] += 1
                act.wait_ge(sum_done, n["norm"])
                root(4, D, half)

            def squares_of(sec):
                two = sec.units == 2 * DT_
                per, base = (2, n["sq"]) if two else (4, n["sq"])

                def body(i, ahead):
                    for t in range(per):
                        if two:
                            ahead(2 * t)
                        last = 2 * t + 1 if two else t
                        act.wait_ge(unit_used, sec.start + RING * i + last + 1)
                        square(bank[2 * t if two else t][:, 0:L], base + t, base + per * i + t)
                        ahead(last)
                rounds(act, sec, body, split_hi)
                n["sq"] += DT_

            def swiglu():
                sec_in, sec_out = next(take), next(take)
                base, at_start = n["sg"], uses_at[sec_in.name_key]

                def body(i, ahead):
                    first = isinstance(i, int) and i == 0
                    if first:
                        ahead(0)
                        ahead(1)
                        input_root()
                        nc.scalar.preload_act_table(ACT.Silu)
                    for f in range(2):
                        act.wait_ge(bank_free[2 * f], at_start[2 * f] + i + 2)
                        act.wait_ge(hid_ready, base + 2 * i + f + 1)
                        nc.scalar.activation(sg[:, f, :], gs[:, f, :], ACT.Silu).then_inc(sg_ready, 1)
                        if f or not first:
                            ahead(2 * f)
                            ahead(2 * f + 1)
                rounds(act, sec_in, body, split_hi, peel=True)
                n["sg"] += FT
                nc.scalar.preload_act_table(ACT.Sqrt)
                squares_of(sec_out)
                norm_out(True)

            def take_o(count):
                act.wait_ge(o_ready, n["head"] + 1)
                nc.scalar.activation(x_hi[:, n["head"] % NH, :], bank[count][:, 0:L], ACT.Copy).then_inc(ohi_ready, 1)
                n["head"] += 1

            def take_values(dst):
                for g in range(0, 6, 2):
                    act.wait_ge(vt_done, n["vt"] + g + 1)
                    nc.scalar.activation(dst[:, g // 2, 0:512], bank[4 + g % 4][:, :], ACT.Copy).then_inc(bank_free[4 + g % 4], 1)
                n["vt"] += 6

            def stick_breaking():
                sec_q, sec_kv, sec_out = next(take), next(take), next(take)

                def body(i, ahead):
                    for s in range(RING):
                        if s == 2 and isinstance(i, int) and i == 0:
                            input_root()
                        ahead(s)
                rounds(act, sec_q, body, split_hi, peel=True)
                rounds(act, sec_kv, lambda i, ahead: [ahead(s) for s in range(RING)], split_hi)
                nc.scalar.preload_act_table_set("natural_log_exp_and_others")
                take_values(vt)
                base = n["mhead"]

                def softplus_parts(hd):
                    z = hd % 2
                    act.wait_ge(zneg_ready, base + hd + 1)
                    nc.scalar.activation(zexp[:, z, :], zneg[:, z, :], ACT.Exp).then_inc(zexp_ready, 1)
                    act.wait_ge(zexp_ready, base + hd + 1)
                    if hd >= 2:
                        act.wait_ge(zsp_ready, base + hd - 1)
                    nc.scalar.activation(zln[:, z, :], zexp[:, z, :], ACT.Ln, bias=one_col).then_inc(zln_ready, 1)

                softplus_parts(0)
                for hd in range(NH + 1):
                    if hd + 1 < NH:
                        softplus_parts(hd + 1)
                    if hd < NH:
                        act.wait_ge(r_ready, base + hd + 1)
                        if hd >= 2:
                            act.wait_ge(o_ready, n["head"])
                        b = z_banks[hd % 4]
                        nc.scalar.activation(prob[:, hd % 2, :], bank[b][:, 0:CAUSAL], ACT.Exp).then_inc(bank_free[b], 1)
                    if hd >= 1:
                        take_o(6 + (hd - 1) % 2)
                n["mhead"] += NH
                nc.scalar.preload_act_table(ACT.Sqrt)
                squares_of(sec_out)
                norm_out(False)

            def take_tiles(sec, per_unit, dst):
                def body(i, ahead):
                    for s in range(RING):
                        for t in range(per_unit * s, per_unit * s + per_unit):
                            if t % 2 == 0:
                                act.wait_ge(unit_used, sec.start + s + 1)
                                nc.scalar.activation(dst(t), bank[t % 4][:, 0:L], ACT.Copy).then_inc(bank_free[t % 4], 1)
                        ahead(s)
                rounds(act, sec, body, split_hi)

            def latent_attention():
                s_in, s_uq, s_ukv, sec_out = (next(take) for _ in range(4))

                for i, (sec, at) in enumerate(((s_in, 1), (s_uq, 0))):
                    split_hi(sec, at, 0)
                    if i == 0:
                        split_hi(sec, at, 1)
                        input_root()
                    for t in range(3):
                        if i or t:
                            split_hi(sec, at, t + 1)
                        g = 3 * i + t
                        if g < 5:
                            act.wait_ge(bank_free[g % 4], uses_at["latents"][g % 4] + g // 4 + 2)
                            square(lat[:, g, :], n["sq"] + g, n["sq"] + g)
                n["sq"] += 5
                finish_norm(3, 384, n["sq"] - 2)
                finish_norm(2, 256, n["sq"], 3, 4)
                take_tiles(s_uq, 3, lambda t: mq[:, t, :] if t < NH else qr[:, t - NH, :])
                take_tiles(s_ukv, 4, lambda t: mk[:, t, :] if t < NH else mv[:, t - NH, :])
                nc.scalar.preload_act_table(ACT.Exp)
                take_values(mvt)

                def exps(hd):
                    act.wait_ge(ntop_ready, hd + 1)
                    z = hd % 2
                    for g, (dst, src) in enumerate(((pa[:, z, 0:128], bank[4 + z][:, 0:128]),
                                                    (pa[:, z, 128:384], bank[4 + z][:, 128:384]),
                                                    (pb[:, z, :], bank[6 + z][:, 0:384]))):
                        last = nc.scalar.activation(dst, src, ACT.Exp, bias=ntop[:, z, g:g + 1], scale=MLA_SCALE,
                                                    accum_out=tot[:, z, g:g + 1])
                    last.then_inc(exp_ready, 1)

                exps(0)
                exps(1)
                for hd in range(NH):
                    act.wait_ge(pT_done, hd + 1)
                    if hd >= 2:
                        act.wait_ge(o_ready, n["head"])
                    nc.scalar.activation(pT[:, hd % 2, :], bank[hd % 2][:, 0:CAUSAL], ACT.Copy).then_inc(bank_free[hd % 2], 1)
                    if hd + 2 < NH:
                        exps(hd + 2)
                    if hd:
                        take_o(2 + (hd - 1) % 2)
                take_o(2 + (NH - 1) % 2)
                nc.scalar.preload_act_table(ACT.Sqrt)
                squares_of(sec_out)
                norm_out(False)

            def time_mixing():
                def parts_of_mix(after_unit):
                    act.wait_ge(unit_used, after_unit)
                    for k in range(DT_):
                        n["xm"] += 1
                        act.wait_ge(xm_ready, n["xm"])
                        nc.scalar.activation(x_hi[:, k, :], xm[:, k % 2, :], ACT.Copy).then_inc(xhi_ready, 1)

                n["xm"] = 0
                for dst in (r_, k_, v_):
                    sec = next(take)
                    parts_of_mix(sec.start)

                    def body(i, ahead):
                        for s in range(RING):
                            if s % 2 == 0:
                                act.wait_ge(unit_used, sec.start + RING * i + s + 1)
                                nc.scalar.activation(dst[:, RING * i + s, 0:L], bank[s][:, 0:L], ACT.Copy).then_inc(bank_free[s], 1)
                            ahead(s)
                    rounds(act, sec, body, split_hi)
                sec1, sec2, sec_out = next(take), next(take), next(take)
                for what in range(3):
                    parts_of_mix(sec1.start + what)
                nc.scalar.preload_act_table_set("sigmoid_and_others")

                def body(i, ahead):
                    for s, f in enumerate((ACT.Tanh, ACT.Copy, ACT.Sigmoid, ACT.Sigmoid)):
                        act.wait_ge(unit_used, sec1.start + s + 1)
                        nc.scalar.activation(lt[:, s, :], bank[s][:, 0:L], f).then_inc(lt_ready, 1)
                        act.wait_ge(lt_ready, s + 1)
                        nc.scalar.activation(lr_hi[:, s, :], lt[:, s, :], ACT.Copy).then_inc(lhi_ready, 1)
                        ahead(s)
                rounds(act, sec1, body, split_hi)

                def body(i, ahead):
                    for s in range(2):
                        for j in range(DT_):
                            act.wait_ge(tile_done, DT_ * s + j + 1)
                            nc.scalar.activation((w_, a_)[s][:, j, 0:L], bank[j % 4][:, 0:L], ACT.Sigmoid,
                                                 bias=vecs[:, V_W0 + DT_ * s + j:V_W0 + DT_ * s + j + 1]).then_inc(bank_free[j % 4], 1)
                        ahead(s)
                    ahead(2)
                    ahead(3)
                rounds(act, sec2, body, split_hi)
                act.wait_ge(kkraw_ready, 1)
                nc.scalar.activation(ex[:, :, :], m[:, :, :], ACT.Square).then_inc(kksq_ready, 1)
                act.wait_ge(kkmax_ready, 1)
                nc.scalar.activation(ex[:, :, :], ex2[:, :, :], ACT.Sqrt, scale=64.0).then_inc(kkroot_ready, 1)
                act.wait_ge(csprev_ready, 1)
                nc.scalar.activation(ex[:, :, :], ex[:, :, :], ACT.Exp).then_inc(pprev_ready, 1)
                nc.scalar.activation(ex2[:, :, :], cs[:, :, :], ACT.Exp, scale=-1.0).then_inc(pinv_ready, 1)
                nc.scalar.activation(cs[:, :, :], cs[:, :, :], ACT.Exp).then_inc(pinc_ready, 1)
                for grp in range(GROUPS):
                    for T in range(3):
                        act.wait_ge(tok_done, 6 * grp + 2 * T + 1)
                        b = rolling["tok", T, 0]
                        nc.scalar.activation(tok[:, T, 0:2, :], bank[b][0:TC, 0:512].rearrange("p (x c) -> p x c", x=2),
                                             ACT.Copy).then_inc(bank_free[b], 1)
                    for pr in range(2):
                        for e in range(2):
                            act.wait_ge(z_done, ZP * (2 * grp + pr) + e + 1)
                            b = rolling["X", pr, e]
                            nc.scalar.activation(inv[:, 2 * pr + e, :], bank[b][0:TC, 0:LP], ACT.Copy).then_inc(bank_free[b], 1)
                        for lv in range(1, 5):
                            for e in range(2):
                                act.wait_ge(y_done, 8 * (2 * grp + pr) + 2 * (lv - 1) + e + 1)
                                b = rolling["Y", pr, lv, e]
                                nc.scalar.activation(yl[:, e, :], bank[b][0:TC, 0:LP], ACT.Copy).then_inc(bank_free[b], 1)
                    for c in range(9):
                        T, rows, count = c // 3, slice(CH * (c % 3), CH * (c % 3) + CH), 9 * grp + c
                        act.wait_ge(sa_done, count + 1)
                        nc.scalar.activation(sa[rows, T, :], bank[3][rows, 0:256], ACT.Copy).then_inc(sa_ready, 1)
                    for pp in range(2):
                        act.wait_ge(out_done, 2 * grp + pp + 1)
                        nc.scalar.activation(v_[:, 2 * grp + pp, 0:L], bank[pp][:, 0:L], ACT.Copy).then_inc(bank_free[pp], 1)
                nc.scalar.preload_act_table(ACT.Sqrt)
                for k in range(DT_):
                    act.wait_ge(yc_ready, k + 1)
                    nc.scalar.activation(ysq[:, k % 2, :], yc[:, k % 2, :], ACT.Square).then_inc(ysq_ready, 1)
                    act.wait_ge(var_done, k + 1)
                    nc.scalar.activation(ystd[:, k % 2, :], bank[2 + k % 2][:, 0:L], ACT.Sqrt, bias=ln_eps_col).then_inc(ystd_ready, 1)
                    act.wait_ge(yg_ready, k + 1)
                    nc.scalar.activation(x_hi[:, k, :], yg[:, k % 2, :], ACT.Copy).then_inc(xhi_ready, 1)
                squares_of(sec_out)
                norm_out(False)

            for s in range(RING):
                split_hi(secs[0], 0, s, first=True)
            for at, layer in enumerate(layers):
                if at == 0:
                    act.wait_ge(loaded, 64)
                gained(layer, 0, at == 0)
                swiglu()
                if layer % 3 == 2:
                    residual_norm_in()
                else:
                    gained(layer, 1)
                (stick_breaking, latent_attention, time_mixing)[layer % 3]()
                gained(layer, 2)
                swiglu()

        @block.gpsimd
        def _(pool):
            n = dict(apply=0, xhi=0)
            take = iter(secs)

            def split_lo(sec, i, s, first=False):
                u = sec.start + RING * i + s
                pool.wait_ge(hi_ready, u + 1)
                w = slice(0, sec.blocks * P)
                nc.gpsimd.tensor_tensor(w_lo[:, s, w], raw[:, s, w], w_hi[:, s, w], ALU.subtract).then_inc(lo_ready, 1)

            def split_section():
                def body(i, ahead):
                    for s in range(RING):
                        ahead(s)
                rounds(pool, next(take), body, split_lo)

            def add_residual():
                for k in range(DT_):
                    n["apply"] += 1
                    pool.wait_ge(apply_ready, n["apply"])
                    nc.gpsimd.tensor_tensor(h[:, k, :], h[:, k, :], m[:, k, :], ALU.add).then_inc(h_ready, 1)

            def low_parts(count, k0=0):
                for k in range(k0, k0 + count):
                    n["xhi"] += 1
                    pool.wait_ge(xhi_ready, n["xhi"])
                    nc.gpsimd.tensor_tensor(x_lo[:, k, :], m[:, k, :], x_hi[:, k, :], ALU.subtract).then_inc(x_ready, 1)

            def low_parts_of(src):
                for k in range(DT_):
                    n["xhi"] += 1
                    pool.wait_ge(xhi_ready, n["xhi"])
                    nc.gpsimd.tensor_tensor(x_lo[:, k, :], src[:, k % 2, :], x_hi[:, k, :], ALU.subtract).then_inc(x_ready, 1)

            def time_mixing():
                for name in "rkv":
                    low_parts_of(xm)
                    split_section()
                for what in range(3):
                    low_parts_of(xm)

                def body(i, ahead):
                    for s in range(RING):
                        pool.wait_ge(lhi_ready, s + 1)
                        nc.gpsimd.tensor_tensor(lr_lo[:, s, :], lt[:, s, :], lr_hi[:, s, :], ALU.subtract).then_inc(bank_free[s], 1)
                        ahead(s)
                rounds(pool, next(take), body, split_lo)
                split_section()
                pool.wait_ge(ops_ready, 1)
                for grp in range(GROUPS):
                    for pr in range(2):
                        for lv in range(1, 5):
                            for e in range(2):
                                at = 4 * grp + 2 * pr
                                pool.wait_ge(am_ready, at + e + 1)
                                if lv > 1 or grp or pr:
                                    pool.wait_ge(y_done, 2 * (2 * at) + 2 * (lv - 2) + e + 1)
                                nc.gpsimd.tensor_tensor(t3(aml[:, e, :]), t3(am[:, e, :]), tri3(m_level[lv]),
                                                        ALU.mult).then_inc(aml_ready, 1)
                    for c in range(8):
                        pool.wait_ge(state_ready, 9 * grp + c + 1)
                        for pp in range(2):
                            col, end = slice(P * pp, P * pp + P), pend[:, 2 * grp + pp, c:c + 1]
                            nc.gpsimd.tensor_scalar_mul(gate[:, col], pair_mask, end)
                            last = nc.gpsimd.tensor_scalar_mul(spre[:, col], state[:, col], end)
                        last.then_inc(spre_ready, 1)
                low_parts_of(yg)
                split_section()

            for s in range(RING):
                split_lo(secs[0], 0, s, first=True)
            for at, layer in enumerate(layers):
                split_section()
                split_section()
                add_residual()
                if layer % 3 == 0:
                    split_section()
                    split_section()
                    split_section()
                elif layer % 3 == 1:
                    split_section()
                    low_parts(3)
                    low_parts(2, 3)
                    split_section()
                    split_section()
                    split_section()
                else:
                    time_mixing()
                add_residual()
                split_section()
                split_section()
                add_residual()

        @block.vector
        def _(dve):
            steps = Steps(dve, dve_chain)
            n = dict(sq=0, sg=0, std=0, head=0, mhead=0, vt=0, xf=0, x=0, gained=0, hsq=0)
            take = iter(secs)

            def inverse_root(dst=rstd[:, :]):
                n["std"] += 1
                dve.wait_ge(std_ready, n["std"])
                steps.link(nc.vector.reciprocal(dst, std[:, :]))

            def low_part(layer, sub, k):
                n["gained"] += 1
                n["x"] += 1
                dve.wait_ge(hg_hi_ready, n["gained"])
                nc.vector.scalar_tensor_tensor(x_lo[:, k, :], h[:, k, :], gain(layer, sub, 0, k), x_hi[:, k, :], ALU.mult,
                                               ALU.subtract).then_inc(x_ready, 1)

            def input_norm():
                n["hsq"] += 1
                dve.wait_ge(hsq_ready, n["hsq"])
                nc.vector.tensor_reduce(acc[:, :], m[:, :, :].rearrange("p t l -> p l t"), AX.X, ALU.add).then_inc(hacc_ready, 1)
                inverse_root(xr)

            def normed(dst, b, ins_scale=None):
                if ins_scale:
                    last = nc.vector.scalar_tensor_tensor(dst, bank[b][:, 0:L], ins_scale, xr, ALU.mult, ALU.mult)
                else:
                    last = nc.vector.tensor_tensor(dst, bank[b][:, 0:L], xr, ALU.mult)
                last.then_inc(bank_free[b], 1)

            def norm_in(tiles, gain_of, k0=0):
                inverse_root()
                n["xf"] += len(tiles)
                n["x"] += len(tiles)
                for k, src in enumerate(tiles):
                    nc.vector.scalar_tensor_tensor(m[:, k0 + k, :], src, gain_of(k), rstd[:, :], ALU.mult,
                                                   ALU.mult).then_inc(xf_ready, 1)

            def residual_norm_in(layer, sub):
                n["sq"] += DT_
                norm_in([h[:, k, :] for k in range(DT_)], lambda k: gain(layer, sub, 0, k))

            def last_product(sec, layer, sub, then=None):
                two = sec.units == 2 * DT_
                per, base = (2 if two else 4), n["sq"]
                steps.link(nc.vector.memset(acc[:, :], 0.0))

                def body(i, ahead):
                    for t in range(per):
                        b = 2 * t if two else t
                        dve.wait_ge(sq_ready, base + per * i + t + 1)
                        nc.vector.tensor_copy(m[:, per * i + t, :], bank[b][:, 0:L]).then_inc(bank_free[b], 1)
                        dve.wait_ge(sq_free, base + per * i + t + 2)
                        nc.vector.tensor_tensor(acc[:, :], acc[:, :], sq[:, (base + t) % 2, :], ALU.add).then_inc(sq_free, 1)
                rounds(dve, sec, body, lambda *a: None)
                n["sq"] += DT_
                inverse_root()
                for k in range(DT_):
                    nc.vector.scalar_tensor_tensor(m[:, k, :], m[:, k, :], gain(layer, sub, 1, k), rstd[:, :], ALU.mult,
                                                   ALU.mult).then_inc(apply_ready, 1)
                    if then and k >= LAG:
                        low_part(*then, k - LAG)
                if then:
                    for k in range(DT_ - LAG, DT_):
                        low_part(*then, k)
                    input_norm()

            def swiglu(layer, sub, then):
                sec_in, sec_out = next(take), next(take)
                base, at_start = n["sg"], uses_at[sec_in.name_key]

                def body(i, ahead):
                    for f in range(2):
                        k = base + 2 * i + f
                        dve.wait_ge(unit_used, sec_in.start + RING * i + 2 * f + 1)
                        normed(gs[:, f, :], 2 * f)
                        dve.wait_ge(unit_used, sec_in.start + RING * i + 2 * f + 2)
                        normed(up[:, f, :], 2 * f + 1)
                        dve.wait_ge(bank_free[2 * f + 1], at_start[2 * f + 1] + i + 2)
                        dve.wait_ge(sg_ready, k + 1)
                        nc.vector.tensor_tensor(hid[:, f, :], sg[:, f, :], up[:, f, :], ALU.mult).then_inc(hid_made, 1)
                        dve.wait_ge(hid_made, k + 1)
                        nc.vector.tensor_copy(hid_hi[:, 2 * i + f, :], hid[:, f, :]).then_inc(hhi_made, 1)
                        dve.wait_ge(hhi_made, k + 1)
                        nc.vector.tensor_tensor(hid_lo[:, 2 * i + f, :], hid[:, f, :], hid_hi[:, 2 * i + f, :],
                                                ALU.subtract).then_inc(hid_ready, 1)
                rounds(dve, sec_in, body, lambda *a: None)
                n["sg"] += FT
                last_product(sec_out, layer, sub, then)

            def take_o(b):
                dve.wait_ge(ohi_ready, n["head"] + 1)
                hd = n["head"] % NH
                nc.vector.tensor_tensor(x_lo[:, hd, :], bank[b][:, 0:L], x_hi[:, hd, :], ALU.subtract).then_inc(bank_free[b], 1)
                n["head"] += 1

            def take_values(dst):
                for g in range(1, 6, 2):
                    dve.wait_ge(vt_done, n["vt"] + g + 1)
                    nc.vector.tensor_copy(dst[:, g // 2, 512:1024], bank[4 + g % 4][:, :]).then_inc(bank_free[4 + g % 4], 1)
                n["vt"] += 6

            def stick_breaking(layer):
                sec_q, sec_kv, sec_out = next(take), next(take), next(take)
                for sec, at, scale in ((sec_q, 0, SB_SCALE), (sec_kv, 8, None)):
                    def body(i, ahead):
                        for s in range(RING):
                            dve.wait_ge(unit_used, sec.start + RING * i + s + 1)
                            normed(qkv[:, at + RING * i + s, :], s, scale)
                    rounds(dve, sec, body, lambda *a: None)
                take_values(vt)
                base = n["mhead"]

                def softplus(hd):
                    z = hd % 2
                    dve.wait_ge(z_ready, base + hd + 1)
                    if hd >= 2:
                        dve.wait_ge(zsp_ready, base + hd - 1)
                    nc.vector.tensor_copy(zraw[:, z, :], bank[z_banks[hd % 4]][:, 0:CAUSAL]).then_inc(zraw_ready, 1)
                    dve.wait_ge(zraw_ready, base + hd + 1)
                    if hd >= 2:
                        dve.wait_ge(zexp_ready, base + hd - 1)
                    nc.vector.scalar_tensor_tensor(zneg[:, z, :], zraw[:, z, :], -1.0, zraw[:, z, :], ALU.mult,
                                                   ALU.min).then_inc(zneg_ready, 1)
                    dve.wait_ge(zln_ready, base + hd + 1)
                    if hd >= 2:
                        dve.wait_ge(r_ready, base + hd - 1)
                    nc.vector.scalar_tensor_tensor(zsp[:, z, :], zraw[:, z, :], 0.0, zln[:, z, :], ALU.max,
                                                   ALU.add).then_inc(zsp_ready, 1)

                softplus(0)
                for hd in range(NH + 1):
                    if hd + 1 < NH:
                        softplus(hd + 1)
                    if hd >= 1:
                        take_o(6 + (hd - 1) % 2)
                n["mhead"] += NH
                last_product(sec_out, layer, 1, (layer, 2))

            def take_tiles(sec, per_unit, dst):
                for t in range(1, RING * per_unit, 2):
                    dve.wait_ge(unit_used, sec.start + t // per_unit + 1)
                    nc.vector.tensor_copy(dst(t), bank[t % 4][:, 0:L]).then_inc(bank_free[t % 4], 1)

            def latent_attention(layer):
                s_in, s_uq, s_ukv, sec_out = (next(take) for _ in range(4))
                for hd in range(NH):
                    half = slice(64, 128) if hd % 2 == 0 else slice(0, 64)
                    nc.vector.memset(qz[half, hd, :], 0.0)
                for t in range(6):
                    dve.wait_ge(unit_used, s_in.start + (2, 3, 4, 6, 7, 8)[t])
                    normed(lat[:, t, :], t % 4)
                n["sq"] += 5
                norm_in([lat[:, k, :] for k in range(3)], lambda k: vecs[:, k:k + 1])
                norm_in([lat[:, k, :] for k in range(3, 5)], lambda k: vecs[:, 3 + k:4 + k], 3)
                take_tiles(s_uq, 3, lambda t: mq[:, t, :] if t < NH else qr[:, t - NH, :])
                take_tiles(s_ukv, 4, lambda t: mk[:, t, :] if t < NH else mv[:, t - NH, :])
                for t in range(5):
                    b, src = 4 + t % 4, (qr[:, t, :] if t < 4 else lat[:, 5, :])
                    dve.wait_ge(rot_ready, t + 1)
                    steps.link(nc.vector.tensor_tensor(rtmp[:, 0, :], bank[b][:, 0:L], sin2, ALU.mult))
                    steps.link(nc.vector.tensor_tensor(rtmp[:, 1, :], src, cos2, ALU.mult))
                    if t < 4:
                        for hf in range(2):
                            p = slice(64 * hf, 64 * hf + 64)
                            last = nc.vector.tensor_tensor(qz[p, 2 * t + hf, :], rtmp[p, 0, :], rtmp[p, 1, :], ALU.add)
                        last.then_inc(bank_free[b], 1)
                    else:
                        nc.vector.tensor_tensor(kr[:, :], rtmp[:, 0, :], rtmp[:, 1, :], ALU.add).then_inc(bank_free[b], 1)
                    dve.wait_ge(bank_free[b], uses_at["rope"][b] + 2 + t // 4)
                take_values(mvt)

                def tops(hd):
                    z = hd % 2
                    dve.wait_ge(zq_ready, hd + 1)
                    nc.vector.reduce_max(top[:, z, 0:1], bank[4 + z][:, 0:128], AX.X)
                    nc.vector.reduce_max(top[:, z, 1:2], bank[4 + z][:, 128:384], AX.X)
                    steps.link(nc.vector.reduce_max(top[:, z, 2:3], bank[6 + z][:, 0:384], AX.X))
                    nc.vector.tensor_scalar_mul(ntop[:, z, :], top[:, z, :], -MLA_SCALE).then_inc(ntop_ready, 1)

                tops(0)
                tops(1)
                for hd in range(NH):
                    z = hd % 2
                    dve.wait_ge(exp_ready, hd + 1)
                    steps.link(nc.vector.reciprocal(rtot[:, z, :], tot[:, z, :]))
                    nc.vector.tensor_scalar_mul(pa[:, z, 0:128], pa[:, z, 0:128], rtot[:, z, 0:1]).then_inc(bank_free[4 + z], 1)
                    nc.vector.tensor_scalar_mul(pa[:, z, 128:384], pa[:, z, 128:384], rtot[:, z, 1:2]).then_inc(bank_free[6 + z], 1)
                    nc.vector.tensor_scalar_mul(pb[:, z, :], pb[:, z, :], rtot[:, z, 2:3]).then_inc(p_ready, 1)
                    if hd + 2 < NH:
                        tops(hd + 2)
                    if hd:
                        take_o(2 + (hd - 1) % 2)
                take_o(2 + (NH - 1) % 2)
                last_product(sec_out, layer, 1, (layer, 2))

            def time_mixing(layer):
                one = lambda c: vecs[:, c:c + 1]
                wide = lambda c: bc(vecs[:, c:c + DT_], L)

                def mix(which):
                    for k in range(DT_):
                        n["xm"] += 1
                        dve.wait_ge(x_ready, n["x"] + n["xm"] - 2) if n["x"] + n["xm"] > 2 else None
                        nc.vector.scalar_tensor_tensor(xm[:, k % 2, :], xx[:, k, :], one(V_MIX + DT_ * which + k), m[:, k, :],
                                                       ALU.mult, ALU.add).then_inc(xm_ready, 1)

                n["xm"] = 0
                dve.wait_ge(xf_ready, n["xf"])
                nc.vector.tensor_tensor(xx[:, :, 1:L], m[:, :, 0:L - 1], m[:, :, 1:L], ALU.subtract)
                steps.link(nc.vector.tensor_scalar_mul(xx[:, :, 0:1], m[:, :, 0:1], -1.0))
                for which, dst in enumerate((r_, k_, v_)):
                    mix(which)
                    sec = next(take)

                    def body(i, ahead):
                        for s in (1, 3):
                            dve.wait_ge(unit_used, sec.start + RING * i + s + 1)
                            nc.vector.tensor_copy(dst[:, RING * i + s, 0:L], bank[s][:, 0:L]).then_inc(bank_free[s], 1)
                    rounds(dve, sec, body, lambda *a: None)
                for which in (3, 4, 5):
                    mix(which)
                sec1, sec2, sec_out = next(take), next(take), next(take)
                for j in range(DT_):
                    if j % 4 == 3:
                        dve.wait_ge(unit_used, sec2.start + 3 + j // 4)
                    else:
                        dve.wait_ge(tile_done, 14 + 3 * (j // 4) + j % 4 + 1)
                    nc.vector.tensor_copy(g_[:, j, :], bank[j % 4][:, 0:L]).then_inc(bank_free[j % 4], 1)
                for x in (r_, k_, w_, a_, v_):
                    last = nc.vector.memset(x[:, :, L:LP], 0.0)
                steps.link(last)
                nc.vector.tensor_tensor(m[:, :, :], k_[:, :, 0:L], wide(V_KK), ALU.mult).then_inc(kkraw_ready, 1)
                dve.wait_ge(rwc_loaded, 16)
                steps.link(nc.vector.tensor_scalar_mul(w_[:, :, 0:L], w_[:, :, 0:L], -float(np.exp(-0.5))))
                for k in range(DT_):
                    last = nc.vector.tensor_tensor_scan(cs[:, k, :], restart, w_[:, k, 0:L], 0.0, ALU.mult, ALU.add)
                steps.link(last)
                for k in range(DT_):
                    dve.wait_ge(head_sum, k + 1)
                    last = nc.vector.tensor_scalar_max(ex2[:, k, :], bank[k][:, 0:L], 1e-24 / 64)
                    last.then_inc(bank_free[k], 1)
                dve.wait_ge(bank_free[DT_ - 1], uses_at["kk"][DT_ - 1] + 2)
                steps.link(nc.vector.memset(pad1[:, :], 0.0))
                nc.vector.memset(pad1[:, :], 0.0).then_inc(kkmax_ready, 1)
                dve.wait_ge(kkroot_ready, 1)
                steps.link(nc.vector.reciprocal(ex[:, :, :], ex[:, :, :]))
                steps.link(nc.vector.tensor_tensor(m[:, :, :], m[:, :, :], ex[:, :, :], ALU.mult))
                nc.vector.tensor_tensor(ex[:, :, :], cs[:, :, :], w_[:, :, 0:L], ALU.subtract).then_inc(csprev_ready, 1)
                dve.wait_ge(pprev_ready, 1)
                steps.link(nc.vector.scalar_tensor_tensor(w_[:, :, 0:L], m[:, :, :], -1.0, ex[:, :, :], ALU.mult, ALU.mult))
                steps.link(nc.vector.scalar_tensor_tensor(ex[:, :, :], a_[:, :, 0:L], -1.0, wide(V_KA), ALU.add, ALU.mult))
                steps.link(nc.vector.scalar_tensor_tensor(k_[:, :, 0:L], ex[:, :, :], 1.0, k_[:, :, 0:L], ALU.add, ALU.mult))
                steps.link(nc.vector.tensor_tensor(a_[:, :, 0:L], a_[:, :, 0:L], m[:, :, :], ALU.mult))
                dve.wait_ge(pinv_ready, 1)
                steps.link(nc.vector.tensor_tensor(a_[:, :, 0:L], a_[:, :, 0:L], ex2[:, :, :], ALU.mult))
                steps.link(nc.vector.tensor_tensor(ex[:, :, :], r_[:, :, 0:L], k_[:, :, 0:L], ALU.mult))
                nc.vector.tensor_tensor(ex[:, :, :], ex[:, :, :], wide(V_RK), ALU.mult).then_inc(bonus_ready, 1)
                steps.link(nc.vector.tensor_tensor(k_[:, :, 0:L], k_[:, :, 0:L], ex2[:, :, :], ALU.mult))
                dve.wait_ge(pinc_ready, 1)
                steps.link(nc.vector.tensor_tensor(r_[:, :, 0:L], r_[:, :, 0:L], cs[:, :, :], ALU.mult))
                for k in range(DT_):
                    dve.wait_ge(head_sum, DT_ + k + 1)
                    nc.vector.scalar_tensor_tensor(m[:, k, :], bank[k][:, 0:L], 64.0, v_[:, k, 0:L], ALU.mult,
                                                   ALU.mult).then_inc(bank_free[k], 1)
                nc.vector.tensor_copy(pend[:, :, :], cs[:, :, CH - 1:CH * 8:CH]).then_inc(ops_ready, 1)
                for grp in range(GROUPS):
                    group(grp)
                for k in range(DT_):
                    e = k % 2
                    dve.wait_ge(mean_done, k + 1)
                    nc.vector.tensor_tensor(yc[:, e, :], v_[:, k, 0:L], bank[e][:, 0:L], ALU.subtract).then_inc(yc_ready, 1)
                    dve.wait_ge(ystd_ready, k + 1)
                    steps.link(nc.vector.reciprocal(yrs[:, e, :], ystd[:, e, :]))
                    nc.vector.scalar_tensor_tensor(yn[:, e, :], yc[:, e, :], one(V_LNW + k), yrs[:, e, :], ALU.mult,
                                                   ALU.mult).then_inc(bank_free[e], 1)
                    dve.wait_ge(bank_free[e], uses_at["ln"][e] + 2 + k // 2)
                    nc.vector.scalar_tensor_tensor(yn[:, e, :], yn[:, e, :], one(V_LNB + k), m[:, k, :], ALU.add,
                                                   ALU.add).then_inc(bank_free[2 + e], 1)
                    dve.wait_ge(bank_free[2 + e], uses_at["ln"][2 + e] + 2 + k // 2)
                    if n["x"] + n["xm"] + k >= 2:
                        dve.wait_ge(x_ready, n["x"] + n["xm"] + k - 1)
                    nc.vector.tensor_tensor(yg[:, e, :], yn[:, e, :], g_[:, k, :], ALU.mult).then_inc(yg_ready, 1)
                n["x"] += n["xm"] + DT_
                last_product(sec_out, layer, 1, (layer, 2))

            def group(grp):
                for T in range(3):
                    dve.wait_ge(tok_done, 6 * grp + 2 * T + 2)
                    b = rolling["tok", T, 1]
                    nc.vector.tensor_copy(tok[:, T, 2, :], bank[b][0:TC, 0:256]).then_inc(bank_free[b], 1)
                for pr in range(2):
                    at = 4 * grp + 2 * pr
                    for e in range(2):
                        q, heads = 2 * pr + e, at + e
                        take3 = lambda x: t3(bank[rolling[x, pr, e]][0:TC, 0:LP])
                        free = lambda ins, x: ins.then_inc(bank_free[rolling[x, pr, e]], 1)
                        dve.wait_ge(gram_done, 4 * heads + 1)
                        nc.vector.tensor_tensor(t3(am[:, e, :]), take3("A"), tri3(m_lower), ALU.mult).then_inc(am_ready, 1)
                        dve.wait_ge(am_ready, heads + 1)
                        steps.link(nc.vector.tensor_tensor(t3(tinv[:, e, :]), t3(am[:, e, :]), tri3(m_level[0]), ALU.mult))
                        free(nc.vector.tensor_tensor(t3(tinv[:, e, :]), t3(tinv[:, e, :]), tri3(ident[0:TC, 0:TC]), ALU.add), "A")
                        dve.wait_ge(gram_done, 4 * heads + 2)
                        if heads:
                            dve.wait_ge(akv_done, 2 * heads - 1)
                        free(nc.vector.tensor_tensor(t3(ak[:, :]), take3("Ak"), tri3(m_upper), ALU.mult), "Ak")
                        dve.wait_ge(gram_done, 4 * heads + 3)
                        free(nc.vector.tensor_tensor(t3(rb[:, q, :]), take3("Rb"), tri3(m_upper_eq), ALU.mult), "Rb")
                        dve.wait_ge(gram_done, 4 * heads + 4)
                        if heads:
                            dve.wait_ge(akv_done, 2 * heads)
                        free(nc.vector.tensor_tensor(t3(rk[:, :]), take3("Rk"), tri3(m_upper_eq), ALU.mult), "Rk")
                        dve.wait_ge(akv_done, 2 * heads + 1)
                        b = rolling["akv", pr, e]
                        nc.vector.tensor_copy(akv[:, :, 64 * q:64 * q + 64],
                                              bank[b][0:TC, 0:192].rearrange("p (t c) -> p t c", t=3)).then_inc(bank_free[b], 1)
                    for lv in range(1, 5):
                        for e in range(2):
                            q = 2 * pr + e
                            z = ZP * (2 * grp + pr) + 2 + 4 * (lv - 1) + (2 if lv < 4 else 1) * e
                            dve.wait_ge(z_done, z + 1)
                            b = rolling["Z", pr, lv, e]
                            nc.vector.tensor_tensor(inv[:, q, :], inv[:, q, :], bank[b][0:TC, 0:LP], ALU.add).then_inc(bank_free[b], 1)
                            if lv < 4:
                                dve.wait_ge(z_done, z + 2)
                                b = rolling["ZT", pr, lv, e]
                                nc.vector.tensor_tensor(tinv[:, e, :], tinv[:, e, :], bank[b][0:TC, 0:LP],
                                                        ALU.add).then_inc(bank_free[b], 1)
                steps.link(nc.vector.memset(pad1[:, :], 0.0))
                nc.vector.memset(u_[:, :], 0.0)
                steps.link(nc.vector.memset(state[:, :], 0.0))
                nc.vector.memset(pad1[:, :], 0.0).then_inc(state_ready, 1)
                for c in range(9):
                    T, rows, count = c // 3, slice(CH * (c % 3), CH * (c % 3) + CH), 9 * grp + c
                    dve.wait_ge(u_done, count + 1)
                    nc.vector.tensor_tensor(u_[rows, :], bank[2][rows, 0:256], akv[rows, T, :], ALU.add).then_inc(u_ready, 1)
                    if c < 8:
                        dve.wait_ge(s_done, 8 * grp + c + 1)
                        dve.wait_ge(spre_ready, 8 * grp + c + 1)
                        steps.link(nc.vector.tensor_tensor(upd[:, :], bank[4][:, 0:256], gate[:, :], ALU.mult))
                        nc.vector.tensor_tensor(state[:, :], upd[:, :], spre[:, :], ALU.add).then_inc(state_ready, 1)

            dve.wait_ge(loaded, 64)
            for k, src in ((0, ident), (1, consts[:, 4 * P:5 * P]), (2, consts[:, 5 * P:6 * P]), (3, consts[:, 6 * P:7 * P])):
                nc.vector.tensor_copy(cbf[:, P * k:P * k + P], src)
            nc.vector.tensor_copy(strict_tail_bf, consts[:, 7 * P:7 * P + 16]).then_inc(cbf_ready, 1)
            for at, layer in enumerate(layers):
                if at == 0:
                    for k in range(DT_):
                        low_part(layer, 0, k)
                    input_norm()
                swiglu(layer, 0, (layer, 1) if layer % 3 != 2 else None)
                if layer % 3 == 2:
                    residual_norm_in(layer, 1)
                    n["x"] -= DT_
                (stick_breaking, latent_attention, time_mixing)[layer % 3](layer)
                swiglu(layer, 2, (layers[at + 1], 0) if at + 1 < len(layers) else None)


def units(w, blocks):
    n = w.shape[0] // blocks
    return np.ascontiguousarray(w.reshape(n, blocks, P, P).transpose(0, 2, 1, 3)).reshape(n, P, blocks * P)


def blocks_of(w):
    k, n = w.shape
    return w.reshape(k // P, P, n // P, P).transpose(2, 0, 1, 3)


def padded(w, rows, cols):
    out = np.zeros((rows, cols), w.dtype)
    out[:w.shape[0], :w.shape[1]] = w
    return out


def constants():
    i, j = np.arange(P)[:, None], np.arange(P)[None, :]
    f = lambda a: np.asarray(a, np.float32)
    neg = np.float32(NEG)
    tail = np.where((i >= 112) & (i - 112 < j[:, :16]), 0, neg)
    small = np.zeros((P, 8), np.float32)
    small[:, 0], small[:, 1], small[:, 2] = EPS, 4 * EPS, 1.0
    small[:, 3] = LN_EPS
    pos = np.arange(L, dtype=np.float32)
    inv = (np.float32(10000.0) ** (-np.arange(32, dtype=np.float32) / np.float32(32))).astype(np.float32)
    ang = (pos[None, :] * inv[np.arange(P) % 32][:, None]).astype(np.float32)
    rot = np.zeros((P, P), np.float32)
    for c in range(P):
        if c % 64 < 32:
            rot[c + 32, c] = -1.0
        else:
            rot[c - 32, c] = 1.0
    cols = [np.eye(P), np.ones((P, P)), np.where(i >= j, -1.0, 0.0), -np.ones((P, P)),
            np.where(j <= i, 0, neg), np.where((j >= 112) & (j <= i), 0, neg), np.where(i < j, 0, neg),
            tail, small, np.cos(ang), np.sin(ang), rot]
    return np.ascontiguousarray(np.concatenate([f(c) for c in cols], 1))


def mixing_constants():
    i, j = np.arange(TC)[:, None], np.arange(TC)[None, :]
    same = i // CH == j // CH
    masks = [same & (j < i), same & (i < j), same & (i <= j)]
    masks += [(i >> (lv + 1) == j >> (lv + 1)) & ((i >> lv) % 2 == 1) & ((j >> lv) % 2 == 0) for lv in range(5)]
    out = np.zeros((P, 2 * P + 8 * TC + L), np.float32)
    p, q = np.arange(P)[:, None], np.arange(P)[None, :]
    out[:, 0:P] = np.where(p // 64 == q // 64, 1.0 / 64, 0)
    for k, mk in enumerate(masks):
        out[0:TC, P + TC * k:P + TC * k + TC] = mk
    out[:, P + 8 * TC:2 * P + 8 * TC] = p // 64 == q // 64
    out[:, 2 * P + 8 * TC:] = (np.arange(L) % CH != 0)[None, :]
    return out


def arrays(a, layers=range(DEPTH)):
    a = {k: np.asarray(v) for k, v in a.items()}
    out = {}
    h0 = np.concatenate([a["meta_tokens"], a["x"][0]], 0)
    out["h0"] = np.ascontiguousarray(h0.T.reshape(DT_, P, L).transpose(1, 0, 2))
    out["gains"] = np.ascontiguousarray(a["norm_gains"].reshape(DEPTH * 6 * DT_, P).T)
    out["consts"] = constants()
    col = lambda v: v.reshape(-1, P).T
    names = ("rw_mix", "rw_w0", "rw_a0", "rw_k_k", "rw_k_a", "rw_r_k", "rw_ln_w", "rw_ln_b")
    out["vecs"] = np.ascontiguousarray(np.concatenate([col(a["mla_q_norm"][0]), col(a["mla_kv_norm"][0])] +
                                                      [col(a[k][0].reshape(-1)) for k in names], 1))
    out["rwc"] = mixing_constants()
    w = a["ffn_w_in"].reshape(DEPTH * 2, DT_, P, 2, FT, P).transpose(0, 4, 3, 2, 1, 5)
    out["ffn_in"] = np.ascontiguousarray(w).reshape(DEPTH * 2 * FT * 2, P, DT_ * P)
    w = a["ffn_w_out"].reshape(DEPTH * 2, 2, HALF, P, DT_, P).transpose(0, 4, 1, 3, 2, 5)
    out["ffn_out"] = np.ascontiguousarray(w).reshape(DEPTH * 2 * DT_ * 2, P, HALF * P)
    flat = lambda w: blocks_of(w).reshape(-1, P, P)
    out["sb_in"] = units(np.concatenate([flat(w) for w in a["sb_w_in"]]), 8)
    out["sb_out"] = units(np.concatenate([flat(w) for w in a["sb_w_out"]]), 8)
    w = a["mla_w_in"][0]
    out["mla_in"] = units(flat(np.concatenate([w, w[:, 640:704]], 1)), 6)
    w = a["mla_w_uq"][0].reshape(384, NH, 192)
    out["mla_uq"] = units(flat(np.concatenate([w[:, :, :128].reshape(384, -1), w[:, :, 128:].reshape(384, -1)], 1)), 9)
    w = a["mla_w_ukv"][0].reshape(256, NH, 256)
    out["mla_ukv"] = units(flat(np.concatenate([w[:, :, :128].reshape(256, -1), w[:, :, 128:].reshape(256, -1)], 1)), 8)
    out["mla_out"] = units(flat(a["mla_w_out"][0]), 8)
    out["rw_in"] = units(np.concatenate([flat(w) for w in a["rw_w_in"][0]]), 8)
    out["rw_lora1"] = units(np.concatenate([flat(padded(a["rw_w1"][0], D, P)), flat(padded(a["rw_a1"][0], D, P)),
                                            flat(padded(a["rw_g1"][0], D, 2 * P))]), 8)
    out["rw_lora2"] = units(np.concatenate([flat(padded(a["rw_w2"][0], P, D)), flat(padded(a["rw_a2"][0], P, D)),
                                            flat(padded(a["rw_g2"][0], 2 * P, D))]), 8)
    out["rw_out"] = units(flat(a["rw_w_out"][0]), 8)
    return out


def kernel(**inputs):
    import concourse.bacc as bacc
    from concourse.bass_utils import run_bass_kernel_spmd

    nc = bacc.Bacc("TRN2", target_bir_lowering=False, num_devices=1)
    given = {f"in_{k}": v for k, v in arrays(inputs).items()}
    A = {k[3:]: nc.dram_tensor(k, v.shape, F32, kind="ExternalInput").ap() for k, v in given.items()}
    out = nc.dram_tensor("out", (P, DT_, SEQ), F32, kind="ExternalOutput").ap()
    build(nc, A, out, list(range(DEPTH)))
    r = run_bass_kernel_spmd(nc, [given], core_ids=[0])
    y = r.results[0]["out"]
    return np.ascontiguousarray(y.transpose(2, 1, 0)).reshape(1, SEQ, D)
```
